# Optimizing a Trainium2 kernel written in Bass

```python
import numpy as np
import jax
import jax.numpy as jnp
from jax import lax
import math
import jax, jax.numpy as jnp

D_MODEL = 1024
BATCH = 1
SEQ = 512
DEPTH = 1

NSA_HEADS = 8
NSA_KV_GROUPS = 2
NSA_GROUP = NSA_HEADS // NSA_KV_GROUPS
NSA_HEAD_DIM = 64
ROPE_DIM = NSA_HEAD_DIM // 4
ROPE_THETA = 500000.0
CMP_BLOCK = 32
CMP_STRIDE = 16
CMP_HIDDEN = 256
SLC_BLOCK = 64
SLC_TOPK = 16
WINDOW = 512
Q_BLOCK = 128

RET_HEADS = 4
RET_QK_DIM = 128
RET_V_DIM = 256
RET_CHUNK = 128
RET_ROPE_THETA = 10000.0

D_FF = 2816
CONV_WIDTH = 3

EPS = 1e-6
NEG = -1e30

NSA_Q_W = NSA_HEADS * NSA_HEAD_DIM
NSA_KV_W = NSA_KV_GROUPS * NSA_HEAD_DIM
RET_QK_W = RET_HEADS * RET_QK_DIM
RET_V_W = RET_HEADS * RET_V_DIM
IN_SPLITS = (NSA_Q_W, 6 * NSA_KV_W, 3 * NSA_HEADS, RET_QK_W, RET_QK_W, RET_V_W, RET_V_W, 2 * D_MODEL)
IN_PROJ_W = sum(IN_SPLITS)


def rms_norm(x, w):
    xf = x.astype(jnp.float32)
    y = xf * lax.rsqrt(jnp.mean(xf * xf, axis=-1, keepdims=True) + EPS)
    return (y * w.astype(jnp.float32)).astype(x.dtype)

def rope(x, rot_dim, theta):
    S = x.shape[1]
    half = rot_dim // 2
    inv = jnp.power(jnp.float32(theta), -jnp.arange(half, dtype=jnp.float32) / half)
    ang = jnp.arange(S, dtype=jnp.float32)[:, None] * inv[None, :]
    cos = jnp.cos(ang)[None, :, None, :]
    sin = jnp.sin(ang)[None, :, None, :]
    xr = x[..., :rot_dim].astype(jnp.float32)
    x1, x2 = xr[..., :half], xr[..., half:]
    rot = jnp.concatenate([x1 * cos - x2 * sin, x1 * sin + x2 * cos], axis=-1).astype(x.dtype)
    return jnp.concatenate([rot, x[..., rot_dim:]], axis=-1)

def masked_softmax(s, mask):
    p = jax.nn.softmax(jnp.where(mask, s, NEG), axis=-1)
    return jnp.where(mask, p, 0.0)

def nsa_attention(q, k_cmp, v_cmp, k_slc, v_slc, k_win, v_win, gates,
                  pe_k, w1_k, w2_k, pe_v, w1_v, w2_v):
    B, S = q.shape[0], q.shape[1]
    H, G, dh = NSA_KV_GROUPS, NSA_GROUP, NSA_HEAD_DIM
    scale = dh ** -0.5
    pos = jnp.arange(S)
    qg = q.reshape(B, S, H, G, dh)

    n_cmp = (S - CMP_BLOCK) // CMP_STRIDE + 1
    cmp_start = np.arange(n_cmp) * CMP_STRIDE
    cmp_idx = cmp_start[:, None] + np.arange(CMP_BLOCK)[None, :]

    def compress(t, pe, w1, w2):
        blk = t[:, cmp_idx] + pe[:, None, :]
        blk = jnp.swapaxes(blk, 2, 3).reshape(B, n_cmp, H, CMP_BLOCK * dh)
        return jax.nn.gelu(blk @ w1) @ w2

    kc = compress(k_cmp, pe_k, w1_k, w2_k)
    vc = compress(v_cmp, pe_v, w1_v, w2_v)
    s_cmp = jnp.einsum('bshgd,bchd->bhgsc', qg, kc).astype(jnp.float32) * scale
    mask_cmp = jnp.asarray(cmp_start + CMP_BLOCK - 1)[None, :] <= pos[:, None]
    p_cmp = masked_softmax(s_cmp, mask_cmp)
    o_cmp = jnp.einsum('bhgsc,bchd->bshgd', p_cmp.astype(vc.dtype), vc)

    n_slc = S // SLC_BLOCK
    slc_start = np.arange(n_slc) * SLC_BLOCK
    overlap = np.clip(np.minimum(cmp_start[:, None] + CMP_BLOCK, slc_start[None, :] + SLC_BLOCK)
                      - np.maximum(cmp_start[:, None], slc_start[None, :]), 0, None) / CMP_BLOCK
    imp = jnp.einsum('bhgsc,cj->bhsj', p_cmp, jnp.asarray(overlap, dtype=jnp.float32))
    cur = (pos // SLC_BLOCK)[:, None]
    jb = jnp.arange(n_slc)[None, :]
    forced = (jb == 0) | (jb == cur) | (jb == cur - 1)
    valid = jb <= cur
    imp = jnp.where(forced, jnp.inf, jnp.where(valid, imp, -jnp.inf))
    top_n = min(SLC_TOPK, n_slc)
    _, sel = lax.top_k(imp, top_n)

    k_blocks = jnp.swapaxes(k_slc.reshape(B, n_slc, SLC_BLOCK, H, dh), 1, 3)
    k_blocks = jnp.swapaxes(k_blocks, 2, 3)
    v_blocks = jnp.swapaxes(jnp.swapaxes(v_slc.reshape(B, n_slc, SLC_BLOCK, H, dh), 1, 3), 2, 3)
    n_q = S // Q_BLOCK
    q_chunks = jnp.moveaxis(qg.reshape(B, n_q, Q_BLOCK, H, G, dh), 1, 0)
    sel_chunks = jnp.moveaxis(sel.reshape(B, H, n_q, Q_BLOCK, top_n), 2, 0)
    pos_chunks = pos.reshape(n_q, Q_BLOCK)
    gather = jax.vmap(jax.vmap(lambda blocks, ix: blocks[ix]))

    def selected_block(args):
        qb, ib, tb = args
        kg = gather(k_blocks, ib)
        vg = gather(v_blocks, ib)
        s = jnp.einsum('bqhgd,bhqnkd->bhgqnk', qb, kg).astype(jnp.float32) * scale
        kpos = ib[..., None] * SLC_BLOCK + jnp.arange(SLC_BLOCK)
        mask = (kpos <= tb[None, None, :, None, None]).reshape(B, H, 1, Q_BLOCK, top_n * SLC_BLOCK)
        p = masked_softmax(s.reshape(B, H, G, Q_BLOCK, top_n * SLC_BLOCK), mask)
        return jnp.einsum('bhgqm,bhqmd->bqhgd', p.astype(vg.dtype),
                          vg.reshape(B, H, Q_BLOCK, top_n * SLC_BLOCK, dh))

    o_slc = lax.map(selected_block, (q_chunks, sel_chunks, pos_chunks))
    o_slc = jnp.moveaxis(o_slc, 0, 1).reshape(B, S, H, G, dh)

    kw = jnp.pad(k_win, ((0, 0), (WINDOW, 0), (0, 0), (0, 0)))
    vw = jnp.pad(v_win, ((0, 0), (WINDOW, 0), (0, 0), (0, 0)))
    band_len = Q_BLOCK + WINDOW
    band = np.arange(n_q)[:, None] * Q_BLOCK + np.arange(band_len)[None, :]
    kb = kw[:, band]
    vb = vw[:, band]
    qb = qg.reshape(B, n_q, Q_BLOCK, H, G, dh)
    s_win = jnp.einsum('bnqhgd,bnkhd->bnhgqk', qb, kb).astype(jnp.float32) * scale
    qi = np.arange(Q_BLOCK)[:, None]
    ki = np.arange(band_len)[None, :]
    k_abs = np.arange(n_q)[:, None, None] * Q_BLOCK + ki[None] - WINDOW
    win_mask = ((ki > qi) & (ki <= qi + WINDOW))[None] & (k_abs >= 0)
    p_win = masked_softmax(s_win, jnp.asarray(win_mask)[None, :, None, None])
    o_win = jnp.einsum('bnhgqk,bnkhd->bnqhgd', p_win.astype(vb.dtype), vb).reshape(B, S, H, G, dh)

    g = gates.reshape(B, S, H, G, 3)
    o = g[..., 0:1] * o_cmp + g[..., 1:2] * o_slc + g[..., 2:3] * o_win
    return o.reshape(B, S, NSA_HEADS * dh)

def retention(q, k, v):
    B, S, H, dk = q.shape
    dv = v.shape[-1]
    C = RET_CHUNK
    n = S // C
    f32 = jnp.float32
    q = rope(q, dk, RET_ROPE_THETA).astype(f32)
    k = rope(k, dk, RET_ROPE_THETA).astype(f32) * (dk ** -0.5)
    v = v.astype(f32)
    log_gamma = jnp.log1p(-jnp.exp2(-5.0 - jnp.arange(H, dtype=f32)))
    idx = jnp.arange(C, dtype=f32)
    diff = idx[:, None] - idx[None, :]
    decay_in = jnp.where(diff >= 0, jnp.exp(log_gamma[:, None, None] * jnp.maximum(diff, 0.0)), 0.0)
    q_decay = jnp.exp(log_gamma[None, :] * (idx[:, None] + 1.0))
    k_decay = jnp.exp(log_gamma[None, :] * (C - 1.0 - idx[:, None]))
    chunk_decay = jnp.exp(log_gamma * C)
    qc = q.reshape(B, n, C, H, dk)
    kc = k.reshape(B, n, C, H, dk)
    vc = v.reshape(B, n, C, H, dv)
    scores = jnp.einsum('bnihd,bnjhd->bnhij', qc, kc) * decay_in
    o_inner = jnp.einsum('bnhij,bnjhe->bnihe', scores, vc)

    def step(state, xs):
        qn, kn, vn = xs
        cross = jnp.einsum('bihd,bhde->bihe', qn, state) * q_decay[None, :, :, None]
        state = state * chunk_decay[None, :, None, None] + jnp.einsum(
            'bjhd,bjhe->bhde', kn * k_decay[None, :, :, None], vn)
        return state, cross

    state0 = jnp.zeros((B, H, dk, dv), f32)
    _, o_cross = lax.scan(step, state0, (jnp.moveaxis(qc, 1, 0), jnp.moveaxis(kc, 1, 0), jnp.moveaxis(vc, 1, 0)))
    o = o_inner + jnp.moveaxis(o_cross, 0, 1)
    return o.reshape(B, S, H, dv)

def head_group_norm(o, w):
    mean = jnp.mean(o, axis=-1, keepdims=True)
    var = jnp.mean(jnp.square(o - mean), axis=-1, keepdims=True)
    return (o - mean) * lax.rsqrt(var + EPS) * w.astype(jnp.float32)

def causal_dwconv(u, w, b):
    S = u.shape[1]
    up = jnp.pad(u, ((0, 0), (CONV_WIDTH - 1, 0), (0, 0)))
    y = b
    for j in range(CONV_WIDTH):
        y = y + w[j] * up[:, j:j + S]
    return y

def first_inputs(seed: int = 0) -> dict:
    key = jax.random.key(seed)
    ks = jax.random.split(key, 20)
    f32 = jnp.float32
    L = DEPTH

    def nrm(k, shape, fan_in):
        return jax.random.normal(k, shape, f32) * (fan_in ** -0.5)

    def gain(k, shape):
        return 1.0 + 0.02 * jax.random.normal(k, shape, f32)

    return {
        'x': jax.random.normal(ks[0], (BATCH, SEQ, D_MODEL), f32),
        'norm_mix_w': gain(ks[1], (L, D_MODEL)),
        'w_in': nrm(ks[2], (L, D_MODEL, IN_PROJ_W), D_MODEL),
        'cmp_pe_k': 0.02 * jax.random.normal(ks[3], (L, CMP_BLOCK, NSA_HEAD_DIM), f32),
        'cmp_w1_k': nrm(ks[4], (L, CMP_BLOCK * NSA_HEAD_DIM, CMP_HIDDEN), CMP_BLOCK * NSA_HEAD_DIM),
        'cmp_w2_k': nrm(ks[5], (L, CMP_HIDDEN, NSA_HEAD_DIM), CMP_HIDDEN),
        'cmp_pe_v': 0.02 * jax.random.normal(ks[6], (L, CMP_BLOCK, NSA_HEAD_DIM), f32),
        'cmp_w1_v': nrm(ks[7], (L, CMP_BLOCK * NSA_HEAD_DIM, CMP_HIDDEN), CMP_BLOCK * NSA_HEAD_DIM),
        'cmp_w2_v': nrm(ks[8], (L, CMP_HIDDEN, NSA_HEAD_DIM), CMP_HIDDEN),
        'w_nsa_branch': nrm(ks[9], (L, NSA_Q_W, D_MODEL), NSA_Q_W),
        'ret_gn_w': gain(ks[10], (L, RET_HEADS, RET_V_DIM)),
        'w_ret_branch': nrm(ks[11], (L, RET_V_W, D_MODEL), RET_V_W),
        'w_mix_out': nrm(ks[12], (L, D_MODEL, D_MODEL), D_MODEL),
        'norm_ffn_w': gain(ks[13], (L, D_MODEL)),
        'w_ffn_up': nrm(ks[14], (L, D_MODEL, 2 * D_FF), D_MODEL),
        'ffn_conv_w': nrm(ks[15], (L, CONV_WIDTH, 2 * D_FF), CONV_WIDTH),
        'ffn_conv_b': 0.01 * jax.random.normal(ks[16], (L, 2 * D_FF), f32),
        'w_ffn_down': nrm(ks[17], (L, D_FF, D_MODEL), D_FF),
        'norm_final_w': gain(ks[18], (D_MODEL,)),
    }

def first_block(x, norm_mix_w, w_in, cmp_pe_k, cmp_w1_k, cmp_w2_k, cmp_pe_v, cmp_w1_v, cmp_w2_v,
              w_nsa_branch, ret_gn_w, w_ret_branch, w_mix_out, norm_ffn_w, w_ffn_up, ffn_conv_w,
              ffn_conv_b, w_ffn_down, norm_final_w):
    B, S, _ = x.shape
    split_at = [int(v) for v in np.cumsum(IN_SPLITS)[:-1]]
    for layer in range(DEPTH):
        h = rms_norm(x, norm_mix_w[layer])
        proj = h @ w_in[layer]
        q_nsa, kv_nsa, g_nsa, q_ret, k_ret, v_ret, g_ret, g_merge = jnp.split(proj, split_at, axis=-1)

        q_nsa = rope(q_nsa.reshape(B, S, NSA_HEADS, NSA_HEAD_DIM), ROPE_DIM, ROPE_THETA)
        kv = kv_nsa.reshape(B, S, 6, NSA_KV_GROUPS, NSA_HEAD_DIM)
        k_cmp, v_cmp = kv[:, :, 0], kv[:, :, 1]
        k_slc = rope(kv[:, :, 2], ROPE_DIM, ROPE_THETA)
        v_slc = kv[:, :, 3]
        k_win = rope(kv[:, :, 4], ROPE_DIM, ROPE_THETA)
        v_win = kv[:, :, 5]
        nsa_gates = jax.nn.sigmoid(g_nsa.reshape(B, S, NSA_HEADS, 3))
        o_a = nsa_attention(q_nsa, k_cmp, v_cmp, k_slc, v_slc, k_win, v_win, nsa_gates,
                            cmp_pe_k[layer], cmp_w1_k[layer], cmp_w2_k[layer],
                            cmp_pe_v[layer], cmp_w1_v[layer], cmp_w2_v[layer])
        y_a = o_a @ w_nsa_branch[layer]

        o_r = retention(q_ret.reshape(B, S, RET_HEADS, RET_QK_DIM),
                        k_ret.reshape(B, S, RET_HEADS, RET_QK_DIM),
                        v_ret.reshape(B, S, RET_HEADS, RET_V_DIM))
        o_r = head_group_norm(o_r, ret_gn_w[layer]) * jax.nn.silu(
            g_ret.reshape(B, S, RET_HEADS, RET_V_DIM).astype(jnp.float32))
        y_b = o_r.astype(x.dtype).reshape(B, S, RET_V_W) @ w_ret_branch[layer]

        gate_a, gate_b = jnp.split(jax.nn.sigmoid(g_merge), 2, axis=-1)
        x = x + (gate_a * y_a + gate_b * y_b) @ w_mix_out[layer]

        h = rms_norm(x, norm_ffn_w[layer])
        u = causal_dwconv(h @ w_ffn_up[layer], ffn_conv_w[layer], ffn_conv_b[layer])
        u_gate, u_val = jnp.split(u, 2, axis=-1)
        x = x + (jax.nn.silu(u_gate) * u_val) @ w_ffn_down[layer]
    return rms_norm(x, norm_final_w)


DEPTH_2 = 2

CHUNK = 64
PLE_DIM = 256
MIX_WIDTH = D_MODEL // 2
POOL_WINDOWS = (2, 4, 8, 16)
POOL_GROUPS = len(POOL_WINDOWS)
POOL_GROUP_DIM = MIX_WIDTH // POOL_GROUPS
ATTN_HEADS = 4
ATTN_HEAD_DIM = MIX_WIDTH // (2 * ATTN_HEADS)
ATTN_V_DIM = 2 * ATTN_HEAD_DIM
ATTN_QK_WIDTH = ATTN_HEADS * 2 * ATTN_HEAD_DIM
ATTN_V_WIDTH = ATTN_HEADS * ATTN_V_DIM
N_BRANCHES = 3
D_IN = 4 * MIX_WIDTH + 2 * ATTN_QK_WIDTH + ATTN_V_WIDTH + N_BRANCHES * D_MODEL
D_FF_2 = 4 * D_MODEL
NEG_INF = -1e30


def rms_norm_2(x, g):
    xf = x.astype(jnp.float32)
    y = xf * lax.rsqrt(jnp.mean(xf * xf, axis=-1, keepdims=True) + EPS)
    return (y * g.astype(jnp.float32)).astype(x.dtype)

def multiscale_pool(a, w, scale):
    b_, s_, _ = a.shape
    af = a.astype(jnp.float32).reshape(b_, s_, POOL_GROUPS, POOL_GROUP_DIM)
    cs = jnp.cumsum(af, axis=1)
    t = jnp.arange(s_)
    outs = []
    for g, win in enumerate(POOL_WINDOWS):
        csg = cs[:, :, g]
        prev = jnp.pad(csg, ((0, 0), (win, 0), (0, 0)))[:, :s_]
        cnt = jnp.minimum(t + 1, win).astype(jnp.float32)[None, :, None]
        outs.append((csg - prev) / cnt - af[:, :, g])
    pooled = jnp.stack(outs, axis=2)
    mixed = jnp.einsum('bsgc,gcd->bsgd', pooled, w.astype(jnp.float32))
    return (mixed.reshape(b_, s_, MIX_WIDTH) * scale.astype(jnp.float32)).astype(a.dtype)

def causal_depthwise_conv(z, w):
    c = z.shape[-1]
    return lax.conv_general_dilated(
        z, w[:, None, :].astype(z.dtype), window_strides=(1,),
        padding=[(CONV_WIDTH - 1, 0)], dimension_numbers=('NWC', 'WIO', 'NWC'),
        feature_group_count=c)

def diff_attention(q1, q2, k1, k2, v, lam):
    b_, s_, h_, d_ = q1.shape
    dv = v.shape[-1]
    nb = s_ // Q_BLOCK
    scale = d_ ** -0.5
    k1, k2, v = (t.transpose(0, 2, 1, 3) for t in (k1, k2, v))

    def to_blocks(q):
        return q.reshape(b_, nb, Q_BLOCK, h_, d_).transpose(1, 0, 3, 2, 4)

    key_chunk = jnp.arange(s_) // CHUNK

    def one_block(args):
        qb1, qb2, bi = args
        q_chunk = (bi * Q_BLOCK + jnp.arange(Q_BLOCK)) // CHUNK
        mask = key_chunk[None, :] <= q_chunk[:, None]

        def probs(q, k):
            s = jnp.einsum('bhqd,bhkd->bhqk', q, k).astype(jnp.float32) * scale
            return jax.nn.softmax(jnp.where(mask, s, NEG_INF), axis=-1)

        att = probs(qb1, k1) - lam * probs(qb2, k2)
        return jnp.einsum('bhqk,bhkd->bhqd', att.astype(v.dtype), v)

    out = lax.map(one_block, (to_blocks(q1), to_blocks(q2), jnp.arange(nb)))
    return out.transpose(1, 0, 3, 2, 4).reshape(b_, s_, h_, dv)

def second_inputs(seed: int = 0) -> dict:
    key = jax.random.key(seed)
    ks = jax.random.split(key, 24)
    nrm = lambda k, shape, s: jax.random.normal(k, shape, jnp.float32) * s
    gain = lambda k, shape: 1.0 + 0.1 * jax.random.normal(k, shape, jnp.float32)
    L = DEPTH_2
    return {
        'x': nrm(ks[0], (BATCH, SEQ, D_MODEL), 1.0),
        'p': nrm(ks[1], (DEPTH_2, BATCH, SEQ, PLE_DIM), 1.0),
        'norm_mix_g': gain(ks[2], (L, D_MODEL)),
        'w_in': nrm(ks[3], (L, D_MODEL, D_IN), D_MODEL ** -0.5),
        'pool_w': nrm(ks[4], (L, POOL_GROUPS, POOL_GROUP_DIM, POOL_GROUP_DIM), POOL_GROUP_DIM ** -0.5),
        'pool_scale': gain(ks[5], (L, MIX_WIDTH)),
        'conv_w': nrm(ks[6], (L, CONV_WIDTH, MIX_WIDTH), CONV_WIDTH ** -0.5),
        'q_norm_g': gain(ks[7], (L, ATTN_HEAD_DIM)),
        'k_norm_g': gain(ks[8], (L, ATTN_HEAD_DIM)),
        'lam_q1': nrm(ks[9], (L, ATTN_HEAD_DIM), 0.1),
        'lam_k1': nrm(ks[10], (L, ATTN_HEAD_DIM), 0.1),
        'lam_q2': nrm(ks[11], (L, ATTN_HEAD_DIM), 0.1),
        'lam_k2': nrm(ks[12], (L, ATTN_HEAD_DIM), 0.1),
        'sub_norm_g': gain(ks[13], (L, ATTN_V_DIM)),
        'w_pool_out': nrm(ks[14], (L, MIX_WIDTH, D_MODEL), MIX_WIDTH ** -0.5),
        'w_conv_out': nrm(ks[15], (L, MIX_WIDTH, D_MODEL), MIX_WIDTH ** -0.5),
        'w_attn_out': nrm(ks[16], (L, ATTN_V_WIDTH, D_MODEL), ATTN_V_WIDTH ** -0.5),
        'w_o': nrm(ks[17], (L, D_MODEL, D_MODEL), D_MODEL ** -0.5),
        'norm_mlp_g': gain(ks[18], (L, D_MODEL)),
        'w_up': nrm(ks[19], (L, D_MODEL, D_FF_2), D_MODEL ** -0.5),
        'w_down': nrm(ks[20], (L, D_FF_2, D_MODEL), D_FF_2 ** -0.5),
        'norm_ple_g': gain(ks[21], (L, D_MODEL)),
        'w_ple_gate': nrm(ks[22], (L, D_MODEL, D_MODEL), D_MODEL ** -0.5),
        'w_ple_proj': nrm(ks[23], (L, PLE_DIM, D_MODEL), PLE_DIM ** -0.5),
    }

def second_block(x, p, norm_mix_g, w_in, pool_w, pool_scale, conv_w, q_norm_g, k_norm_g,
              lam_q1, lam_k1, lam_q2, lam_k2, sub_norm_g, w_pool_out, w_conv_out,
              w_attn_out, w_o, norm_mlp_g, w_up, w_down, norm_ple_g, w_ple_gate, w_ple_proj):
    b_, s_, _ = x.shape
    sizes = [MIX_WIDTH, MIX_WIDTH, MIX_WIDTH, MIX_WIDTH,
             ATTN_QK_WIDTH, ATTN_QK_WIDTH, ATTN_V_WIDTH]
    split_at = [int(c) for c in np.cumsum(sizes)]
    h = x
    for i in range(DEPTH_2):
        u = rms_norm_2(h, norm_mix_g[i])
        proj = u @ w_in[i]
        a_in, c_x, c_b, c_c, q, k, v, gates = jnp.split(proj, split_at, axis=-1)

        y_a = multiscale_pool(a_in, pool_w[i], pool_scale[i])

        y_b = c_b * causal_depthwise_conv(c_c * c_x, conv_w[i])

        q = q.reshape(b_, s_, ATTN_HEADS, 2, ATTN_HEAD_DIM)
        k = k.reshape(b_, s_, ATTN_HEADS, 2, ATTN_HEAD_DIM)
        v = v.reshape(b_, s_, ATTN_HEADS, ATTN_V_DIM)
        q1 = rms_norm_2(q[..., 0, :], q_norm_g[i])
        q2 = rms_norm_2(q[..., 1, :], q_norm_g[i])
        k1 = rms_norm_2(k[..., 0, :], k_norm_g[i])
        k2 = rms_norm_2(k[..., 1, :], k_norm_g[i])
        lam_init = 0.8 - 0.6 * math.exp(-0.3 * i)
        lam = (jnp.exp(jnp.sum(lam_q1[i].astype(jnp.float32) * lam_k1[i].astype(jnp.float32)))
               - jnp.exp(jnp.sum(lam_q2[i].astype(jnp.float32) * lam_k2[i].astype(jnp.float32)))
               + lam_init)
        o = diff_attention(q1, q2, k1, k2, v, lam)
        o = rms_norm_2(o, sub_norm_g[i]) * (1.0 - lam_init)
        y_c = o.reshape(b_, s_, ATTN_V_WIDTH)

        g_a, g_b, g_c = jnp.split(jax.nn.sigmoid(gates), N_BRANCHES, axis=-1)
        merged = (g_a * (y_a @ w_pool_out[i])
                  + g_b * (y_b @ w_conv_out[i])
                  + g_c * (y_c @ w_attn_out[i]))
        h = h + merged @ w_o[i]

        m = rms_norm_2(h, norm_mlp_g[i])
        h = h + jnp.square(jax.nn.relu(m @ w_up[i])) @ w_down[i]

        e = rms_norm_2(h, norm_ple_g[i])
        h = h + jax.nn.sigmoid(e @ w_ple_gate[i]) * (p[i] @ w_ple_proj[i])
    return h


def setup_inputs(seed=0):
    out = dict(first_inputs(seed))
    for name, value in second_inputs(seed + 1).items():
        if name != "x":
            out[name + "_2"] = value
    return out


def reference(
    x, norm_mix_w, w_in, cmp_pe_k, cmp_w1_k, cmp_w2_k, cmp_pe_v, cmp_w1_v, cmp_w2_v,
    w_nsa_branch, ret_gn_w, w_ret_branch, w_mix_out, norm_ffn_w, w_ffn_up, ffn_conv_w,
    ffn_conv_b, w_ffn_down, norm_final_w, p_2, norm_mix_g_2, w_in_2, pool_w_2, pool_scale_2,
    conv_w_2, q_norm_g_2, k_norm_g_2, lam_q1_2, lam_k1_2, lam_q2_2, lam_k2_2, sub_norm_g_2,
    w_pool_out_2, w_conv_out_2, w_attn_out_2, w_o_2, norm_mlp_g_2, w_up_2, w_down_2,
    norm_ple_g_2, w_ple_gate_2, w_ple_proj_2,
):
    x = first_block(
        x, norm_mix_w, w_in, cmp_pe_k, cmp_w1_k, cmp_w2_k, cmp_pe_v, cmp_w1_v, cmp_w2_v,
        w_nsa_branch, ret_gn_w, w_ret_branch, w_mix_out, norm_ffn_w, w_ffn_up, ffn_conv_w,
        ffn_conv_b, w_ffn_down, norm_final_w,
    )
    return second_block(
        x, p_2, norm_mix_g_2, w_in_2, pool_w_2, pool_scale_2, conv_w_2, q_norm_g_2, k_norm_g_2,
        lam_q1_2, lam_k1_2, lam_q2_2, lam_k2_2, sub_norm_g_2, w_pool_out_2, w_conv_out_2,
        w_attn_out_2, w_o_2, norm_mlp_g_2, w_up_2, w_down_2, norm_ple_g_2, w_ple_gate_2,
        w_ple_proj_2,
    )


_drawn_inputs = setup_inputs


def setup_inputs(seed=0):
    import zlib

    import numpy as np

    out = dict(_drawn_inputs(seed))
    spreads = {}
    factors = {'cmp_pe_k': 200.0,
     'cmp_pe_v': 8.0,
     'ret_gn_w': 6.121,
     'norm_ffn_w': 2.694,
     'ffn_conv_b': 4.808,
     'lam_k1_2': 5.075,
     'norm_ple_g_2': 3.775}
    for name, (base, spread) in spreads.items():
        noise = np.random.default_rng([zlib.crc32(name.encode()), seed]).standard_normal(out[name].shape)
        drawn = base * np.exp(spread * noise) if base else spread * noise
        out[name] = jnp.asarray(drawn.astype(out[name].dtype))
    for name, factor in factors.items():
        out[name] = (out[name] * factor).astype(out[name].dtype)
    return out
```

```python
from contextlib import ExitStack, contextmanager

import numpy as np

import concourse.bass as bass
from concourse import mybir

F32 = mybir.dt.float32
F32R = mybir.dt.float32r
ALU = mybir.AluOpType
ACT = mybir.ActivationFunctionType
AX = mybir.AxisListType

P = 128
S = 512
QT = S // P
D = 1024
KD = D // P
NEG = -1e30
EPS = 1e-6
UNIT = 8 * P
BLOCK = 2 * UNIT

HEADS, KVG, DH = 8, 2, 64
CMP_BLOCK, CMP_STRIDE, CMP_HIDDEN = 32, 16, 256
NCMP = (S - CMP_BLOCK) // CMP_STRIDE + 1
ROPE_DIM, ROPE_THETA = DH // 4, 500000.0
RH, RDK, RDV, RET_THETA = 4, 128, 256, 10000.0
DFF = 2816
FT = DFF // P
LAYERS = 2
PH = 4
POOL_WINDOWS = (2, 4, 8, 16)
DFF2 = 4096
PLE = 256

NSA_UNITS = 12
CMP_UNITS = 8
RET_UNITS = 8
YA_UNITS = 4
YB_UNITS = 16
MIX_UNITS = 8
FFN_CHUNKS = (8, 8, 6)
U_CMP = NSA_UNITS
U_RET = U_CMP + CMP_UNITS
U_YA = U_RET + RH * RET_UNITS
U_YB = U_YA + YA_UNITS
U_MIX = U_YB + YB_UNITS
U_FFN = U_MIX + MIX_UNITS
U_L = U_FFN + sum(2 * c + 8 for c in FFN_CHUNKS)
L_QK, L_MIX, L_MERGE = 4, 12, 28
L_WO = L_MERGE + 36
L_MLP = L_WO + 8
L_PLE = L_MLP + 64
L_UNITS = L_PLE + 12
UNITS = U_L + LAYERS * L_UNITS
GROUPS = UNITS // 4

C1_MIX, C1_FFN, C1_FIN, C1_GN = 0, 8, 16, 24
C1_CONV = 32
C1_PE = C1_CONV + 2 * FT * 4
C1_W2 = C1_PE + 32
C1_N = C1_W2 + 256
C2_MIX, C2_MLP, C2_PLE = 0, 8, 16
C2_PSCALE, C2_CONV, C2_QG, C2_KG, C2_SUB, C2_LINIT = 24, 28, 40, 41, 42, 43
C2_LAM = 48
C2_POOLW = C2_LAM + 256
C2_N = C2_POOLW + PH * P
PAR_N = max(C1_N, C2_N)

K_ID, K_ONE, K_BD, K_CAUSAL, K_CHUNK = 0, 128, 256, 384, 512
K_CMPA = 640
K_CMPM = K_CMPA + QT * NCMP
K_CNT = K_CMPM + QT * NCMP
K_N = K_CNT + PH * 16
SWAP_NSA = [i + 8 if i < 8 else i - 8 if i < 16 else i for i in range(32)]
N_RET, N_LAYER = 99, 398
POOLED = [1, 0, 1, 0]
SWAP_RET = [(i + 16) % 32 for i in range(32)]


class Count:

    def __init__(self, start=0):
        self.base, self.k = start, 0

    def now(self):
        return self.base + self.k

    def due(self, n=1):
        self.k += n
        return self.now()

    def up(self, n=1):
        self.k += n
        return n


@contextmanager
def repeat(eng, n, rises):
    start = [(t.base, t.k) for t, _ in rises]
    with eng.Fori(0, n) as i:
        for (t, rise), (base, k) in zip(rises, start):
            t.base, t.k = base + i * rise + k, 0
        yield i
        for m, (t, rise) in enumerate(rises):
            assert t.k == rise, (f"count {m} of the loop", t.k, rise)
    for (t, rise), (base, k) in zip(rises, start):
        t.base, t.k = base, k + n * rise


def build(nc, stream, xT, tab, decay, rope, par1, par2, pT, out):
    ctx = ExitStack()
    with ctx:
        def sb(name, shape, dt=F32):
            return ctx.enter_context(nc.sbuf_tensor(name, shape, dt))

        def sem(name):
            return ctx.enter_context(nc.semaphore(name))

        bank = [ctx.enter_context(nc.psum_tensor(f"bank{i}", [P, S], F32)) for i in range(8)]
        b_s0, b_s1, b_cmp, b_o, b_r0, b_r1 = bank[2:8]

        raw = sb("raw", [P, 2, BLOCK])
        w_hi = sb("w_hi", [P, 2, BLOCK], F32R)
        w_lo = sb("w_lo", [P, 2, BLOCK], F32R)
        a_hi = sb("a_hi", [P, KD, S], F32R)
        a_lo = sb("a_lo", [P, KD, S], F32R)
        y_hi = sb("y_hi", [P, 12, S], F32R)
        y_lo = sb("y_lo", [P, 12, S], F32R)
        h = sb("h", [P, KD, S])
        m = sb("m", [P, KD, S])
        par = sb("par", [P, PAR_N])
        cst = sb("cst", [P, K_N])
        rstd = sb("rstd", [P, S])
        ssum = sb("ssum", [P, S])
        ta = sb("ta", [P, 16 + S])
        tb = sb("tb", [P, 16 + S])
        td = sb("td", [P, 16 + S])
        tile_c = sb("tile_c", [P, S])[:, :]
        prob = sb("prob", [P, 2, S])
        pt = sb("pt", [P, 2, S])
        small = sb("small", [P, 64])
        work = sb("work", [P, 9 * S + 288])

        ident = cst[:, K_ID:K_ID + P]
        ones = cst[:, K_ONE:K_ONE + P]
        ones2 = cst[:, K_BD:K_BD + P]
        tile_a, tile_b, tile_d = ta[:, 16:], tb[:, 16:], td[:, 16:]
        eps = small[:, 60:61]
        decay_t = h[:, 0:4, :]
        rope_cn, rope_sn, rope_cr, rope_sr = (h[:, 4 + i, :] for i in range(4))

        def w1(at, n):
            return work[:, at:at + n]
        ks, kw = w1(0, S), w1(S, S)
        vs, vw = (w1((2 + i) * S, S).rearrange("p (a f) -> p a f", f=P) for i in range(2))
        rv = w1(4 * S, 2 * S).rearrange("p (a f) -> p a f", f=RDV)
        rp = w1(6 * S, 1280)
        rg = rp[:, 0:2 * S].rearrange("p (e s) -> p e s", e=2)
        at = 6 * S + 1280
        kc = w1(at, 32)
        vc = w1(at + 32, P)
        gn = w1(at + 160, QT * 24).rearrange("p (i c) -> p i c", c=24)
        hid = w1(at + 256, 128).rearrange("p (k c) -> p k c", c=64)
        pc = w1(at + 384, 32)
        ptc = w1(at + 416, P)
        rq, rk = h[:, 4, :], h[:, 5, :]
        qt = tile_d
        xc_hi = [y_hi[:, 2 * i:2 * i + 2, :].rearrange("p a s -> p (a s)")[:, 0:992]
                 .rearrange("p (m g c) -> p m g c", g=2, c=NCMP) for i in range(2)]
        xc_lo = [y_lo[:, 2 * i:2 * i + 2, :].rearrange("p a s -> p (a s)")[:, 0:992]
                 .rearrange("p (m g c) -> p m g c", g=2, c=NCMP) for i in range(2)]
        xc = rp[:, 0:992].rearrange("p (m g c) -> p m g c", g=2, c=NCMP)
        qn = w1(0, 4 * S).rearrange("p (h s) -> p h s", s=S)
        kn = w1(4 * S, 4 * S).rearrange("p (h s) -> p h s", s=S)
        vn = m[:, 4:8, :].rearrange("p h (a f) -> p h a f", f=P)

        landed = [sem("block_landed_0"), sem("block_landed_1")]
        hi_done = sem("unit_hi_done")
        lo_done = sem("unit_lo_done")
        unit_done = sem("unit_done")
        evac = sem("unit_evacuated")
        x_landed = sem("x_landed")
        constants_landed = sem("constants_landed")
        tables_landed = sem("tables_landed")
        parameters_landed = sem("parameters_landed")
        p_landed = sem("p_landed")
        x_used = sem("x_used")
        tables_used = sem("tables_used")
        parameters_used = sem("parameters_used")
        a_tile_ready = sem("a_tile_ready")
        y_tile_ready = sem("y_tile_ready")
        squares_ready = sem("squares_ready")
        square_sum_done = sem("square_sum_done")
        root_ready = sem("root_ready")
        activated = sem("activated")
        to_activate = sem("to_activate")
        to_transpose = sem("to_transpose")
        transposed = sem("transposed")
        gelu_ready = sem("gelu_ready")
        compressed = sem("compressed")
        scores_ready = sem("scores_ready")
        max_ready = sem("max_ready")
        exp_ready = sem("exp_ready")
        probs_ready = sem("probs_ready")
        probs_transposed = sem("probs_transposed")
        probs_copied = sem("probs_copied")
        values_added = sem("values_added")
        attention_out_read = sem("attention_out_read")
        retention_input_ready = sem("retention_input_ready")
        product_ready = sem("product_ready")
        product_read = sem("product_read")
        vector_step = sem("vector_step")
        out_stored = sem("out_stored")
        wait_placed = sem("wait_placed")

        block = ctx.enter_context(nc.Block())

        def conv_unit_slot(j):
            return (j // 2) % 2, slice((j % 2) * UNIT, (j % 2 + 1) * UNIT)

        @block.sync
        def _(sp):
            for s in range(2):
                sp.dma_start(raw[:, s], stream[s]).then_inc(landed[s], 16)
            with sp.Fori(1, GROUPS) as g:
                for s in range(2):
                    sp.wait_ge(lo_done, g * 4 - 2 + 2 * s)
                    sp.dma_start(raw[:, s], stream[g * 2 + s]).then_inc(landed[s], 16)
            for s in range(2):
                sp.wait_ge(lo_done, GROUPS * 4 - 2 + 2 * s)
                sp.dma_start(raw[:, s], stream[s]).then_inc(landed[s], 16)
            for s in range(2):
                sp.wait_ge(landed[s], 16 * (GROUPS + 1))
            sp.wait_ge(parameters_used, 1 + LAYERS)
            sp.dma_start(out, h[:, :, :]).then_inc(out_stored, 16)
            sp.wait_ge(out_stored, 16)

        @block.gpsimd
        def _(pool):
            with pool.Fori(0, GROUPS) as g:
                for j in range(4):
                    s, cols = conv_unit_slot(j)
                    pool.wait_ge(hi_done, g * 4 + j + 1)
                    pool.tensor_tensor(w_lo[:, s, cols], raw[:, s, cols], w_hi[:, s, cols],
                                       ALU.subtract).then_inc(lo_done, 1)
            for j in range(3):
                s, cols = conv_unit_slot(j)
                pool.wait_ge(hi_done, GROUPS * 4 + j + 1)
                pool.tensor_tensor(w_lo[:, s, cols], raw[:, s, cols], w_hi[:, s, cols],
                                   ALU.subtract).then_inc(lo_done, 1)

        @block.scalar
        def _(act):
            def hi_part(u0, j):
                g4 = u0 + (j // 4) * 4
                j %= 4
                s, cols = conv_unit_slot(j)
                if j % 2 == 0:
                    act.wait_ge(landed[s], g4 * 4 + 16)
                act.wait_ge(unit_done, g4 + (j + 1))
                act.activation(w_hi[:, s, cols], raw[:, s, cols], ACT.Copy).then_inc(hi_done, 1)

            def ahead(u0, j):
                hi_part(u0, j + 3)

            pre, res = Count(), Count()
            sump, root = Count(), Count()
            mx, ex = Count(), Count()
            gelu = Count()
            ptp, ptr, pv = Count(), Count(), Count()

            def tile_root(dst, src, scale):
                act.wait_ge(square_sum_done, sump.due())
                act.activation(dst, src, ACT.Sqrt, bias=eps, scale=scale)\
                    .then_inc(root_ready, root.up())

            act.dma_start(h[:, :, :], xT).then_inc(x_landed, 16)
            act.dma_start(cst[:, :], tab).then_inc(constants_landed, 16)
            act.dma_start(par[:, 0:C1_N], par1).then_inc(parameters_landed, 16)
            for j in range(3):
                hi_part(0, j)
            act.wait_ge(to_activate, pre.due())
            act.wait_ge(x_used, 1)
            act.dma_start(h[:, 0:4, :], decay).then_inc(tables_landed, 16)
            act.dma_start(h[:, 4:8, :], rope).then_inc(tables_landed, 16)
            tile_root(rstd[:, :], b_r1[:, :], 1.0 / D)

            def run(u0, n):
                for j in range(n):
                    ahead(u0, j)

            run(0, NSA_UNITS)
            act.wait_ge(to_activate, pre.due())
            act.activation(gn, gn, ACT.Sigmoid).then_inc(activated, res.up())
            for kv in range(2):
                for n in range(2):
                    for half in range(2):
                        ahead(U_CMP, kv * 4 + n * 2 + half)
                act.wait_ge(to_activate, pre.due())
                act.activation(hid[:, :, 0:62], hid[:, :, 0:62], ACT.Gelu_apprx_tanh)\
                    .then_inc(gelu_ready, gelu.up())

            def softmax_step(parts, last_scale):
                act.wait_ge(max_ready, mx.due())
                for n, (dst, src, b) in enumerate(parts):
                    ins = act.activation(dst, src, ACT.Exp, bias=small[:, b:b + 1], scale=last_scale,
                                         accum_out=small[:, b + 4:b + 5])
                ins.then_inc(exp_ready, ex.up())

            def copy_transposed(parts):
                act.wait_ge(values_added, pv.due())
                act.wait_ge(probs_transposed, ptp.due())
                for dst, src in parts:
                    ins = act.activation(dst, src, ACT.Copy)
                ins.then_inc(probs_copied, ptr.up())

            with repeat(act, RH, [(pre, 1), (res, 1), (mx, 8), (ex, 8), (ptp, 8), (ptr, 8), (pv, 8),
                                  (sump, 1), (root, 1)]) as t:
                u0 = t * RET_UNITS + U_RET
                for j in range(RET_UNITS):
                    i = j % QT
                    n = (i + 1) * P
                    softmax_step([(pc[:, 0:NCMP], b_cmp[:, 0:NCMP], 0),
                                  (prob[:, 0, 0:n], b_s0[:, 0:n], 1),
                                  (prob[:, 1, 0:n], b_s1[:, 0:n], 2)], DH ** -0.5)
                    ahead(u0, j)
                    copy_transposed([(pt[:, 0, 0:n], b_s0[:, 0:n]), (pt[:, 1, 0:n], b_s1[:, 0:n]),
                                     (ptc[0:NCMP, :], b_cmp[0:NCMP, 0:P])])
                    if j == 7:
                        act.wait_ge(to_activate, pre.due())
                        act.activation(rg, rg, ACT.Silu).then_inc(activated, res.up())
                        tile_root(tile_c, b_r1[:, :], 1.0 / RDV)
            act.wait_ge(tables_used, 1)
            act.dma_start(h[:, :, :], xT).then_inc(x_landed, 16)
            act.wait_ge(to_activate, pre.due())
            for half in range(2):
                act.activation(m[:, 4 * half:4 * half + 4, :], m[:, 4 * half:4 * half + 4, :],
                                      ACT.Sigmoid).then_inc(activated, res.up())
            run(U_YA, YA_UNITS)
            for j in range(YB_UNITS):
                ahead(U_YB, j)
                if j % 2 == 0:
                    act.wait_ge(to_activate, pre.due())
                    act.activation(tile_a, tile_a, ACT.Sigmoid).then_inc(activated, res.up())
            run(U_MIX, MIX_UNITS)
            tile_root(rstd[:, :], b_r1[:, :], 1.0 / D)
            u = U_FFN
            for c in FFN_CHUNKS:
                with repeat(act, c // 2, [(pre, 2), (res, 2)]) as b:
                    for j in range(4):
                        ahead(b * 4 + u, j)
                        if j % 2 == 1:
                            act.wait_ge(to_activate, pre.due())
                            act.activation(tile_c, tile_c, ACT.Silu).then_inc(activated, res.up())
                u += 2 * c
                run(u, 8)
                u += 8
            tile_root(rstd[:, :], b_r1[:, :], 1.0 / D)

            with repeat(act, LAYERS, [(pre, 33), (res, 33), (mx, 16), (ex, 16), (ptp, 16), (ptr, 16),
                                      (pv, 16), (sump, 15), (root, 15)]) as layer:
                act.wait_ge(parameters_used, layer + 1)
                act.dma_start(par[:, 0:C2_N], par2[layer]).then_inc(parameters_landed, 16)
                lam = small[:, 16:18]
                act.wait_ge(to_activate, pre.due())
                act.activation(lam, lam, ACT.Exp).then_inc(activated, res.up())
                tile_root(rstd[:, :], b_r1[:, :], 1.0 / D)
                ul = layer * L_UNITS + U_L
                run(ul, 4)
                for j in range(8):
                    ahead(ul + L_QK, j)
                    tile_root(tile_b, b_r0[:, :], 1.0 / 64)
                for j in range(16):
                    i = j % QT
                    n = (i + 1) * P
                    softmax_step([(prob[:, e, 0:n], (b_s0, b_s1)[e][:, 0:n], e) for e in range(2)],
                                 64 ** -0.5)
                    ahead(ul + L_MIX, j)
                    if i == 0 and j > 0:
                        tile_root(ssum[:, :], b_r0[:, :], 1.0 / P)
                    copy_transposed([(pt[:, 0, 0:n], b_s0[:, 0:n])])
                tile_root(ssum[:, :], b_r0[:, :], 1.0 / P)
                with repeat(act, 3, [(pre, 8), (res, 8)]) as br:
                    for half in range(2):
                        for j in range(6):
                            ahead(ul + L_MERGE + br * 12, half * 6 + j)
                            if j < 4:
                                act.wait_ge(to_activate, pre.due())
                                g = work[:, j * S:(j + 1) * S]
                                act.activation(g, g, ACT.Sigmoid).then_inc(activated, res.up())
                run(ul + L_WO, 8)
                tile_root(rstd[:, :], b_r1[:, :], 1.0 / D)
                with repeat(act, 4, []) as c:
                    run(ul + L_MLP + c * 16, 16)
                act.dma_start(prob[:, :, :], pT[layer]).then_inc(p_landed, 16)
                for j in range(12):
                    ahead(ul + L_PLE, j)
                    if j == 3:
                        tile_root(rstd[:, :], b_r1[:, :], 1.0 / D)
                    if j >= 4:
                        act.wait_ge(to_activate, pre.due())
                        act.activation(tile_a, tile_a, ACT.Sigmoid).then_inc(activated, res.up())

        @block.tensor
        def _(pe):
            pe.sem_inc(unit_done, 4)
            pe.sem_inc(values_added, 1)
            a_rdy, y_rdy = Count(), Count()
            sums, sump = Count(), Count()
            tin, tout = Count(), Count()
            cx, cp = Count(), Count()
            score, prb, ptp, ptr, pv = (Count() for _ in range(5))
            ofree = Count()
            rin, rps, rfree = Count(), Count(), Count()

            def product(dst, w, rhs_hi, rhs_lo, nk, first=None, start=True, stop=True):
                s, c0 = w
                for k in range(nk):
                    if first is not None:
                        first(k)
                    cols = slice(c0 + k * P, c0 + (k + 1) * P)
                    pe.matmul(dst, w_hi[:, s, cols], rhs_hi(k), start=start and k == 0, stop=False)
                    pe.matmul(dst, w_hi[:, s, cols], rhs_lo(k), start=False, stop=False)
                    ins = pe.matmul(dst, w_lo[:, s, cols], rhs_hi(k), start=False,
                                    stop=stop and k == nk - 1)
                return ins

            def unit(u0, j, lag, dsts, rhs, nk, first=None, start=True, stop=True):
                s, cols = conv_unit_slot(j)
                pe.wait_ge(lo_done, u0 + (j + 1))
                pe.wait_ge(evac, u0 + (j + 5 - lag))
                hi, lo = rhs
                for o, dst in enumerate(dsts):
                    ins = product(dst, (s, cols.start + o * nk * P), hi, lo, nk,
                                  first if o == 0 else None, start, stop)
                ins.then_inc(unit_done, 1)

            def a_op(n=S):
                return (lambda k: a_hi[:, k, :]), (lambda k: a_lo[:, k, :])

            def y_op(at=0):
                return (lambda k: y_hi[:, at + k, :]), (lambda k: y_lo[:, at + k, :])

            def next_a(k):
                pe.wait_ge(a_tile_ready, a_rdy.due())

            def next_y(k):
                pe.wait_ge(y_tile_ready, y_rdy.due())

            def square_sum(dst=None, w=None, src=None):
                pe.wait_ge(squares_ready, sums.due())
                pe.matmul((b_r1 if dst is None else dst)[:, :], ones if w is None else w,
                                  ssum[:, :] if src is None else src, start=True, stop=True)\
                                      .then_inc(square_sum_done, sump.up())

            def transposes(dst, src, n=QT):
                pe.wait_ge(to_transpose, tin.due())
                for a in range(n):
                    ins = pe.transpose(dst[:, a * P:(a + 1) * P], src[:, a * P:(a + 1) * P], ident)
                ins.then_inc(transposed, tout.up())

            pe.wait_ge(constants_landed, 16)
            def simple(u0, j, banks=2, first=None, nk=8):
                unit(u0, j, banks, [bank[j % banks][:, :]], a_op(), nk, first)
            for j in range(NSA_UNITS):
                simple(0, j, first=next_a if j == 0 else None, nk=8 if j < 11 else 1)
                if j == 0:
                    square_sum()
                if j in (3, 4):
                    transposes(b_r0, tile_c)
            transposes(b_r0, tile_c)
            for kv in range(2):
                pe.wait_ge(y_tile_ready, y_rdy.due())
                for n in range(2):
                    for half in range(2):
                        j = kv * 4 + n * 2 + half
                        lag = 2 if j == 0 else 3 + half
                        unit(U_CMP, j, lag, [bank[n][:, 0:62]],
                             ((lambda k, kv=kv, h_=half: xc_hi[kv][:, 8 * h_ + k].rearrange("p g c -> p (g c)")),
                              (lambda k, kv=kv, h_=half: xc_lo[kv][:, 8 * h_ + k].rearrange("p g c -> p (g c)"))),
                             8, start=half == 0, stop=half == 1)
                pe.wait_ge(gelu_ready, cx.due())
                w2 = par[:, C1_W2 + kv * 128:C1_W2 + (kv + 1) * 128].rearrange("p (k d) -> p k d", d=DH)
                for g in range(KVG):
                    for k in range(2):
                        hc = hid[:, k, g * NCMP:(g + 1) * NCMP]
                        if kv == 0:
                            ins = pe.matmul(b_r0[g * DH:(g + 1) * DH, 0:NCMP], w2[:, k, :], hc,
                                            start=k == 0, stop=k == 1)
                        else:
                            ins = pe.matmul(b_r1[0:NCMP, g * DH:(g + 1) * DH], hc, w2[:, k, :],
                                            start=k == 0, stop=k == 1)
                ins.then_inc(compressed, cp.up())

            with repeat(pe, RH, [(score, 8), (prb, 8), (ptp, 8), (ptr, 8), (pv, 8), (ofree, 1),
                                 (rin, 4), (rps, 9), (rfree, 8), (sums, 1), (sump, 1),
                                 (tin, 1)]) as t:
                u0 = t * RET_UNITS + U_RET
                pe.wait_ge(to_transpose, tin.due())

                def ret_scores(a, dst):
                    pe.matmul(dst[:, 0:S - a * P], rk[:, a * P:(a + 1) * P], rq[:, a * P:S],
                                     start=True, stop=True).then_inc(product_ready, rps.up())

                def ret_transposes(dst, src):
                    pe.wait_ge(retention_input_ready, rin.due())
                    for a in range(QT):
                        ins = pe.transpose(dst[:, a * P:(a + 1) * P], src[:, a * P:(a + 1) * P], ident)
                    ins.then_inc(product_ready, rps.up())

                def ret_values(e, dst):
                    at = 0
                    for a in range(QT):
                        n = S - a * P
                        ins = pe.matmul(dst[:, a * P:S], rv[:, a, e * P:(e + 1) * P], rp[:, at:at + n],
                                        start=a == 0, stop=a == QT - 1, skip_group_check=True)
                        at += n
                    ins.then_inc(product_ready, rps.up())

                for j in range(RET_UNITS):
                    g, i = j // QT, j % QT
                    n = (i + 1) * P
                    rows = slice(g * DH, (g + 1) * DH)
                    q = qt[rows, i * P:(i + 1) * P]
                    pe.matmul(b_cmp[:, 0:NCMP], q, kc[rows, 0:NCMP], start=True, stop=True)
                    pe.matmul(b_s0[:, 0:n], q, ks[rows, 0:n], start=True, stop=True)
                    pe.matmul(b_s1[:, 0:n], q, kw[rows, 0:n], start=True, stop=True)\
                        .then_inc(scores_ready, score.up())
                    unit(u0, j, 2, [bank[j % 2][:, :]], a_op(), 8)
                    pe.wait_ge(probs_ready, prb.due())
                    for a in range(i + 1):
                        pe.transpose(b_s0[:, a * P:(a + 1) * P], prob[:, 0, a * P:(a + 1) * P], ident)
                        pe.transpose(b_s1[:, a * P:(a + 1) * P], prob[:, 1, a * P:(a + 1) * P], ident)
                    pe.transpose(b_cmp[0:NCMP, 0:P], pc[:, 0:NCMP], ident)\
                        .then_inc(probs_transposed, ptp.up())
                    if j == 2:
                        pe.wait_ge(retention_input_ready, rin.due())
                        ret_scores(0, b_r0)
                        ret_scores(1, b_r1)
                    if j == 3:
                        pe.wait_ge(product_read, rfree.due())
                        ret_transposes(b_r0, tile_c)
                        pe.wait_ge(product_read, rfree.due())
                        ret_scores(2, b_r1)
                    if j == 4:
                        pe.wait_ge(product_read, rfree.due())
                        ret_scores(3, b_r0)
                        pe.wait_ge(product_read, rfree.due())
                        ret_transposes(b_r1, tile_b)
                    if j == 5:
                        pe.wait_ge(product_read, rfree.due(2))
                        ret_values(0, b_r0)
                        ret_values(1, b_r1)
                    if j == 6:
                        pe.wait_ge(product_read, rfree.due(2))
                        pe.wait_ge(retention_input_ready, rin.due())
                        pe.matmul(b_r0[:, :], ones, tile_c, start=True, stop=True)\
                            .then_inc(product_ready, rps.up())
                    if j == 7:
                        square_sum()
                    pe.wait_ge(probs_copied, ptr.due())
                    if j == 0:
                        pe.wait_ge(attention_out_read, ofree.due())
                    col = slice(i * P, (i + 1) * P)
                    pe.matmul(b_o[rows, col], vc[0:NCMP, rows], ptc[0:NCMP, :], start=True, stop=False,
                              skip_group_check=True)
                    for a in range(i + 1):
                        pe.matmul(b_o[rows, col], vs[:, a, rows], pt[:, 0, a * P:(a + 1) * P],
                                  start=False, stop=False, skip_group_check=True)
                        ins = pe.matmul(b_o[rows, col], vw[:, a, rows], pt[:, 1, a * P:(a + 1) * P],
                                        start=False, stop=a == i, skip_group_check=True)
                    ins.then_inc(values_added, pv.up())

            first_lags = [2, 3, 3]

            def bank4(j):
                return bank[(j + 2) % 4][:, :]

            def pairs(u0, n, rhs, nk, first=None):
                for j in range(n):
                    unit(u0, j, 2, [bank4(2 * j), bank4(2 * j + 1)], rhs, nk, first if j == 0 else None)

            def singles(u0, n, rhs, nk=8, first=None, lags=()):
                for j in range(n):
                    unit(u0, j, lags[j] if j < len(lags) else 4, [bank4(j)], rhs, nk,
                         first if j == 0 else None)

            pe.wait_ge(y_tile_ready, y_rdy.due(RH * 3))
            pairs(U_YA, YA_UNITS, y_op(8), 4)
            for j in range(YB_UNITS):
                unit(U_YB, j, first_lags[j] if j < 3 else 4, [bank4(j)],
                     a_op() if j % 2 == 0 else y_op(), 8)
            merged = [8, 9, 10, 11, 4, 5, 6, 7]
            singles(U_MIX, MIX_UNITS, ((lambda k: y_hi[:, merged[k], :]), (lambda k: y_lo[:, merged[k], :])),
                    first=next_y)
            square_sum()
            pe.wait_ge(a_tile_ready, a_rdy.due(KD))
            u = U_FFN
            for c in FFN_CHUNKS:
                with repeat(pe, c // 2, []) as b:
                    singles(b * 4 + u, 4, a_op())
                u += 2 * c
                pe.wait_ge(y_tile_ready, y_rdy.due(c))
                singles(u, 8, y_op(), c)
                u += 8
            square_sum()

            with repeat(pe, LAYERS, [(a_rdy, 24), (y_rdy, 54), (sums, 15), (sump, 15), (tin, 8),
                                     (tout, 4), (rin, 4), (rps, 4), (score, 16), (prb, 16),
                                     (ptp, 16), (ptr, 16), (pv, 16), (ofree, 4)]) as layer:
                ul = layer * L_UNITS + U_L
                for j in range(4):
                    simple(ul, j, first=next_a if j == 0 else None)
                    if j == 0:
                        square_sum()
                    else:
                        transposes(b_r0, tile_c)
                for j in range(8):
                    simple(ul + L_QK, j)
                    if j == 0:
                        transposes(b_r0, tile_c)
                    else:
                        square_sum(b_r0, ones2, tile_b)
                for j in range(16):
                    hd, i = j // QT, j % QT
                    n = (i + 1) * P
                    if i == 0:
                        pe.wait_ge(retention_input_ready, rin.due())
                    for e, dst in enumerate((b_s0, b_s1)):
                        rows = slice(64 * e, 64 * (e + 1))
                        ins = pe.matmul(dst[:, 0:n], qn[rows, hd, i * P:(i + 1) * P],
                                        kn[rows, hd, 0:n], start=True, stop=True)
                    ins.then_inc(scores_ready, score.up())
                    simple(ul + L_MIX, j)
                    if j == 0:
                        square_sum(b_r0, ones2, tile_b)
                    elif i == 0:
                        square_sum(b_r0)
                    if 1 <= j <= 4:
                        pe.wait_ge(to_transpose, tin.due())
                        g = j - 1
                        pe.matmul(b_r1[:, :], par[:, C2_POOLW + g * P:C2_POOLW + (g + 1) * P],
                                         (tile_b, tile_d)[POOLED[g]], start=True, stop=True)\
                                             .then_inc(product_ready, rps.up())
                    pe.wait_ge(probs_ready, prb.due())
                    for a in range(i + 1):
                        ins = pe.transpose(b_s0[:, a * P:(a + 1) * P], prob[:, 0, a * P:(a + 1) * P], ident)
                    ins.then_inc(probs_transposed, ptp.up())
                    pe.wait_ge(probs_copied, ptr.due())
                    if i == 0:
                        pe.wait_ge(attention_out_read, ofree.due())
                    for a in range(i + 1):
                        ins = pe.matmul(b_o[:, i * P:(i + 1) * P], vn[:, hd, a, :],
                                        pt[:, 0, a * P:(a + 1) * P], start=a == 0, stop=a == i,
                                        skip_group_check=True)
                    ins.then_inc(values_added, pv.up())
                square_sum(b_r0)
                pe.wait_ge(y_tile_ready, y_rdy.due(12))
                pe.sem_inc(wait_placed, 1)
                with repeat(pe, 3, []) as br:
                    ub = ul + L_MERGE + br * 12
                    for half in range(2):
                        for j in range(4):
                            unit(ub, half * 6 + j, [2, 3, 3, 4][j], [bank4(j)], a_op(), 8)
                        for j in range(2):
                            unit(ub, half * 6 + 4 + j, 3 - j, [bank4(2 * j), bank4(2 * j + 1)],
                                 ((lambda k: y_hi[:, bass.ds(br * 4 + k, 1), :].rearrange("p a s -> p (a s)")),
                                  (lambda k: y_lo[:, bass.ds(br * 4 + k, 1), :].rearrange("p a s -> p (a s)"))), 4)
                singles(ul + L_WO, 8, y_op(), first=next_y, lags=first_lags)
                square_sum()
                pe.wait_ge(a_tile_ready, a_rdy.due(KD))
                pe.sem_inc(wait_placed, 1)
                with repeat(pe, 4, [(y_rdy, 8)]) as c:
                    uc = ul + L_MLP + c * 16
                    singles(uc, 8, a_op())
                    pe.wait_ge(y_tile_ready, y_rdy.due(8))
                    singles(uc + 8, 8, y_op())
                pe.wait_ge(y_tile_ready, y_rdy.due(2))
                pairs(ul + L_PLE, 4, y_op(8), 2)
                singles(ul + L_PLE + 4, 1, a_op(), first=next_a, lags=first_lags)
                square_sum()
                for j in range(1, 8):
                    unit(ul + L_PLE + 4, j, first_lags[j] if j < 3 else 4, [bank4(j)], a_op(), 8)

        @block.vector
        def _(dve):
            V = dve
            V.sem_inc(evac, 4)
            V.sem_inc(attention_out_read, 1)
            steps = Count()
            a_rdy, y_rdy = Count(), Count()
            pre, res, root = Count(), Count(), Count()
            sums = Count()
            tin, tout = Count(), Count()
            cp = Count()
            score, mx, ex, prb, pv = (Count() for _ in range(5))
            pv.k = 1
            ofree = Count(1)
            rin, rps, rfree = Count(), Count(), Count()

            def leave(u0, j, ins):
                ins.then_inc(evac, 1)
                V.wait_ge(evac, u0 + (j + 5))

            def arrive(u0, j):
                V.wait_ge(vector_step, steps.now())
                V.wait_ge(unit_done, u0 + (j + 5))

            def scaled(dst, src, u0, j):
                arrive(u0, j)
                leave(u0, j, V.tensor_tensor(dst, src, rstd[:, :], ALU.mult))

            def split(at, src):
                V.tensor_copy(y_hi[:, at, :], src).then_inc(vector_step, steps.up())
                V.wait_ge(vector_step, steps.now())
                V.tensor_tensor(y_lo[:, at, :], src, y_hi[:, at, :], ALU.subtract)\
                    .then_inc(y_tile_ready, y_rdy.up())
                V.wait_ge(y_tile_ready, y_rdy.now())

            def norm_tile(k, g_col, last):
                g = par[:, g_col + k:g_col + k + 1]
                V.tensor_scalar(a_hi[:, k, :], h[:, k, :], g, None, ALU.mult)\
                    .then_inc(vector_step, steps.up())
                V.wait_ge(vector_step, steps.now())
                V.scalar_tensor_tensor(out=a_lo[:, k, :], in0=h[:, k, :], scalar=g,
                                                in1=a_hi[:, k, :], op0=ALU.mult, op1=ALU.subtract)\
                                                    .then_inc(a_tile_ready, a_rdy.up())
                V.wait_ge(a_tile_ready, a_rdy.now())
                square_tile(k, last)

            def square_tile(k, last):
                V.tensor_tensor(tile_a if k else ssum[:, :], h[:, k, :], h[:, k, :], ALU.mult)\
                    .then_inc(vector_step, steps.up())
                V.wait_ge(vector_step, steps.now())
                if k:
                    ins = V.tensor_tensor(ssum[:, :], ssum[:, :], tile_a, ALU.add)
                    if last:
                        ins.then_inc(squares_ready, sums.up())
                        V.wait_ge(squares_ready, sums.now())
                    else:
                        ins.then_inc(vector_step, steps.up())
                        V.wait_ge(vector_step, steps.now())

            def rms():
                V.wait_ge(root_ready, root.due())
                V.reciprocal(rstd[:, :], rstd[:, :]).then_inc(vector_step, steps.up())
                V.wait_ge(vector_step, steps.now())

            def rope(dst, src, u0, j, swap, cos, sin):
                scaled(tile_a, src, u0, j)
                V.sem_inc(wait_placed, 1)
                V.stream_shuffle(tile_b, tile_a, swap).then_inc(vector_step, steps.up())
                V.wait_ge(vector_step, steps.now())
                V.tensor_tensor(tile_b, tile_b, sin, ALU.mult).then_inc(vector_step, steps.up())
                V.tensor_tensor(tile_a, tile_a, cos, ALU.mult).then_inc(vector_step, steps.up())
                V.wait_ge(vector_step, steps.now())
                return V.tensor_tensor(dst, tile_a, tile_b, ALU.add)

            V.memset(small[:, :], 0.0).then_inc(vector_step, steps.up())
            V.memset(ta[:, 0:16], 0.0).then_inc(vector_step, steps.up())
            V.memset(tb[:, 0:16], 0.0).then_inc(vector_step, steps.up())
            V.memset(td[:, 0:16], 0.0).then_inc(vector_step, steps.up())
            V.wait_ge(vector_step, steps.now())
            V.memset(eps, EPS).then_inc(to_activate, pre.up())
            V.wait_ge(to_activate, pre.now())
            V.wait_ge(x_landed, 16)
            V.wait_ge(parameters_landed, 16)
            for k in range(KD):
                norm_tile(k, C1_MIX, k == KD - 1)
            V.tensor_copy(small[:, 20:21], h[:, 0, 0:1]).then_inc(x_used, 1)
            rms()
            V.wait_ge(constants_landed, 16)
            for kv in range(2):
                scaled(tile_a, bank[kv][:, :], 0, kv)
                t16 = tile_a.rearrange("p (c r) -> p c r", r=CMP_STRIDE)
                for g in range(KVG):
                    for par_ in range(2):
                        for half in range(2):
                            src = t16[g * DH:(g + 1) * DH, half:half + NCMP, par_::2]
                            V.tensor_copy(xc[par_ * DH:(par_ + 1) * DH, 8 * half:8 * half + 8, g, :],
                                               src.rearrange("p c r -> p r c"))\
                                                   .then_inc(vector_step, steps.up())
                V.wait_ge(vector_step, steps.now())
                pe_ = par[:, C1_PE + 16 * kv:C1_PE + 16 * kv + 16]
                xf = xc.rearrange("p m g c -> p m (g c)")
                V.tensor_tensor(xf, xf, pe_.unsqueeze(2).to_broadcast([P, 16, 2 * NCMP]), ALU.add)\
                    .then_inc(vector_step, steps.up())
                V.wait_ge(vector_step, steps.now())
                V.tensor_copy(xc_hi[kv], xc).then_inc(vector_step, steps.up())
                V.wait_ge(vector_step, steps.now())
                V.tensor_tensor(xc_lo[kv], xc, xc_hi[kv], ALU.subtract)\
                    .then_inc(y_tile_ready, y_rdy.up())
                V.wait_ge(y_tile_ready, y_rdy.now())
            for j in (2, 3):
                scaled(tile_c, bank[j % 2][:, :], 0, j)
                V.tensor_copy(small[:, 20:21], tile_c[:, 0:1]).then_inc(to_transpose, tin.up())
                V.wait_ge(to_transpose, tin.now())
                V.wait_ge(transposed, tout.due())
                V.tensor_copy((vs, vw)[j - 2], b_r0[:, :].rearrange("p (a f) -> p a f", f=P))\
                    .then_inc(vector_step, steps.up())
                V.wait_ge(vector_step, steps.now())
            V.wait_ge(tables_landed, 32)
            for j in range(4, 10):
                dst = (ks, kw)[j - 4] if j < 6 else m[:, 4 + j - 6, :]
                rope(dst, bank[j % 2][:, :], 0, j, SWAP_NSA, rope_cn, rope_sn)\
                    .then_inc(vector_step, steps.up())
            scaled(tile_c, bank[0][:, :], 0, 10)
            V.tensor_copy(small[:, 20:21], tile_c[:, 0:1]).then_inc(to_transpose, tin.up())
            V.wait_ge(to_transpose, tin.now())
            arrive(0, 11)
            leave(0, 11, V.tensor_copy(small[:, 21:22], bank[1][:, 0:1]))
            V.wait_ge(transposed, tout.due())
            V.tensor_copy(gn, b_r0[:, :].rearrange("p (i c) -> p i c", c=P)[:, :, 0:24])\
                .then_inc(to_activate, pre.up())
            V.wait_ge(to_activate, pre.now())
            for kv in range(2):
                for n in range(2):
                    arrive(U_CMP, kv * 4 + n * 2 + 1)
                    ins = V.tensor_copy(hid[:, n, 0:62], bank[n][:, 0:62])
                    ins.then_inc(evac, 2)
                    V.wait_ge(evac, U_CMP + kv * 4 + n * 2 + 2 + 4)
                V.tensor_copy(small[:, 20:21], hid[:, 1, 0:1]).then_inc(to_activate, pre.up())
                V.wait_ge(to_activate, pre.now())
                V.wait_ge(compressed, cp.due())
                if kv == 0:
                    V.tensor_copy(kc[:, 0:NCMP], b_r0[:, 0:NCMP]).then_inc(vector_step, steps.up())
                else:
                    V.tensor_copy(vc[0:NCMP, :], b_r1[0:NCMP, 0:P]).then_inc(vector_step, steps.up())
            V.wait_ge(activated, res.due())

            def maxima(parts, scale, masks):
                V.wait_ge(scores_ready, score.due())
                for dst, mask in masks:
                    V.tensor_tensor(dst, dst, mask, ALU.add).then_inc(vector_step, steps.up())
                V.wait_ge(vector_step, steps.now())
                for n, src in enumerate(parts):
                    V.tensor_reduce(small[:, 8 + n:9 + n], src, AX.X, ALU.max)\
                        .then_inc(vector_step, steps.up())
                V.wait_ge(vector_step, steps.now())
                b = len(parts)
                V.tensor_scalar(small[:, 0:b], small[:, 8:8 + b], -scale, None, ALU.mult)\
                    .then_inc(max_ready, mx.up())
                V.wait_ge(max_ready, mx.now())

            causal = cst[:, K_CAUSAL:K_CAUSAL + P]
            with repeat(V, RH, [(steps, N_RET), (score, 8), (mx, 8), (ex, 8), (prb, 8), (pv, 8),
                                (ofree, 1), (rin, 4), (rps, 9), (rfree, 8), (sums, 1), (root, 1),
                                (pre, 1), (res, 1), (y_rdy, 3), (tin, 1)]) as t:
                u0 = t * RET_UNITS + U_RET
                V.tensor_copy(qt, m[:, bass.ds(t + 4, 1), :].rearrange("p a s -> p (a s)"))\
                    .then_inc(to_transpose, tin.up())
                V.wait_ge(to_transpose, tin.now())
                dec = decay_t[:, bass.ds(t, 1), :].rearrange("p a s -> p (a s)")
                p_at = [0, 512, 896, 1152, 1280]

                def decayed(a, src):
                    n = S - a * P
                    V.wait_ge(product_ready, rps.due())
                    V.tensor_tensor(rp[:, p_at[a]:p_at[a + 1]], src[:, 0:n], dec[:, 0:n], ALU.mult)\
                        .then_inc(product_read, rfree.up())
                    V.wait_ge(product_read, rfree.now())

                for j in range(RET_UNITS):
                    g, i = j // QT, j % QT
                    n = (i + 1) * P
                    diag = slice(i * P, n)
                    maxima([b_cmp[:, 0:NCMP], b_s0[:, 0:n], b_s1[:, 0:n]], DH ** -0.5,
                           [(b_cmp[:, 0:NCMP], cst[:, K_CMPA + i * NCMP:K_CMPA + (i + 1) * NCMP]),
                            (b_s0[:, diag], causal), (b_s1[:, diag], causal)])
                    V.wait_ge(exp_ready, ex.due())
                    V.reciprocal(small[:, 12:15], small[:, 4:7]).then_inc(vector_step, steps.up())
                    V.wait_ge(vector_step, steps.now())
                    V.tensor_tensor(small[:, 12:15], small[:, 12:15],
                                         gn[:, i, bass.ds(t * 3 + 12 * g, 3)], ALU.mult)\
                                             .then_inc(vector_step, steps.up())
                    V.wait_ge(vector_step, steps.now())
                    V.scalar_tensor_tensor(out=pc[:, 0:NCMP], in0=pc[:, 0:NCMP], scalar=small[:, 12:13],
                                                in1=cst[:, K_CMPM + i * NCMP:K_CMPM + (i + 1) * NCMP],
                                                op0=ALU.mult, op1=ALU.mult)\
                                                    .then_inc(vector_step, steps.up())
                    V.tensor_scalar(prob[:, 0, 0:n], prob[:, 0, 0:n], small[:, 13:14], None, ALU.mult)\
                        .then_inc(vector_step, steps.up())
                    V.tensor_scalar(prob[:, 1, 0:n], prob[:, 1, 0:n], small[:, 14:15], None, ALU.mult)\
                        .then_inc(probs_ready, prb.up())
                    V.wait_ge(probs_ready, prb.now())
                    src = bank[j % 2][:, :]
                    if j == 0:
                        rope(rq, src, u0, j, SWAP_RET, rope_cr, rope_sr)\
                            .then_inc(vector_step, steps.up())
                    elif j == 1:
                        rope(rk, src, u0, j, SWAP_RET, rope_cr, rope_sr)\
                            .then_inc(retention_input_ready, rin.up())
                        V.wait_ge(retention_input_ready, rin.now())
                    elif j in (2, 3):
                        dst = tile_c if j == 2 else tile_b
                        scaled(dst, src, u0, j)
                        V.tensor_copy(small[:, 20:21], dst[:, 0:1])\
                            .then_inc(retention_input_ready, rin.up())
                        V.wait_ge(retention_input_ready, rin.now())
                    elif j < 6:
                        scaled(m[:, bass.ds(t * 2 + (j - 4), 1), :].rearrange("p a s -> p (a s)"), src, u0, j)
                    else:
                        scaled(rg[:, j - 6, :], src, u0, j)
                    if j == 7:
                        V.tensor_copy(small[:, 20:21], rg[:, 1, 0:1]).then_inc(to_activate, pre.up())
                        V.wait_ge(to_activate, pre.now())
                    if j == 2:
                        decayed(0, b_r0)
                        decayed(1, b_r1)
                    elif j == 3:
                        V.wait_ge(product_ready, rps.due())
                        V.tensor_copy(rv[:, :, 0:P], b_r0[:, :].rearrange("p (a f) -> p a f", f=P))\
                            .then_inc(product_read, rfree.up())
                        V.wait_ge(product_read, rfree.now())
                        decayed(2, b_r1)
                    elif j == 4:
                        decayed(3, b_r0)
                        V.wait_ge(product_ready, rps.due())
                        V.tensor_copy(rv[:, :, P:RDV], b_r1[:, :].rearrange("p (a f) -> p a f", f=P))\
                            .then_inc(product_read, rfree.up())
                        V.wait_ge(product_read, rfree.now())
                    elif j == 5:
                        V.wait_ge(product_ready, rps.due())
                        V.tensor_copy(rq, b_r0[:, :]).then_inc(product_read, rfree.up())
                        V.wait_ge(product_read, rfree.now())
                        V.wait_ge(product_ready, rps.due())
                        V.tensor_copy(rk, b_r1[:, :]).then_inc(product_read, rfree.up())
                        V.wait_ge(product_read, rfree.now())
                        V.wait_ge(product_read, rfree.now())
                        V.tensor_tensor(tile_c, rq, rk, ALU.add)\
                            .then_inc(retention_input_ready, rin.up())
                        V.wait_ge(retention_input_ready, rin.now())
                    elif j == 6:
                        V.wait_ge(product_ready, rps.due())
                        for o in (rq, rk):
                            V.scalar_tensor_tensor(out=o, in0=b_r0[:, :], scalar=-1.0 / RDV, in1=o,
                                                        op0=ALU.mult, op1=ALU.add)\
                                                            .then_inc(vector_step, steps.up())
                        V.wait_ge(vector_step, steps.now())
                        V.tensor_tensor(tile_a, rq, rq, ALU.mult).then_inc(vector_step, steps.up())
                        V.tensor_tensor(ssum[:, :], rk, rk, ALU.mult).then_inc(vector_step, steps.up())
                        V.wait_ge(vector_step, steps.now())
                        V.tensor_tensor(ssum[:, :], ssum[:, :], tile_a, ALU.add)\
                            .then_inc(squares_ready, sums.up())
                        V.wait_ge(squares_ready, sums.now())
                V.wait_ge(activated, res.due())
                V.wait_ge(root_ready, root.due())
                V.reciprocal(tile_c, tile_c).then_inc(vector_step, steps.up())
                V.wait_ge(vector_step, steps.now())
                for e, o in enumerate((rq, rk)):
                    tile = t * 2 + e
                    V.scalar_tensor_tensor(out=o, in0=o, scalar=par[:, bass.ds(tile + C1_GN, 1)],
                                                in1=tile_c, op0=ALU.mult, op1=ALU.mult)\
                                                    .then_inc(vector_step, steps.up())
                    V.wait_ge(vector_step, steps.now())
                    V.tensor_tensor(o, o, rg[:, e, :], ALU.mult).then_inc(vector_step, steps.up())
                    V.wait_ge(vector_step, steps.now())
                    hi = y_hi[:, bass.ds(tile, 1), :].rearrange("p a s -> p (a s)")
                    V.tensor_copy(hi, o).then_inc(vector_step, steps.up())
                    V.wait_ge(vector_step, steps.now())
                    V.tensor_tensor(y_lo[:, bass.ds(tile, 1), :].rearrange("p a s -> p (a s)"),
                                             o, hi, ALU.subtract).then_inc(y_tile_ready, y_rdy.up())
                    V.wait_ge(y_tile_ready, y_rdy.now())
                V.wait_ge(values_added, pv.due(8))
                V.tensor_copy(tile_a, b_o[:, :]).then_inc(attention_out_read, ofree.up())
                V.wait_ge(attention_out_read, ofree.now())
                V.wait_ge(attention_out_read, ofree.now())
                hi = y_hi[:, bass.ds(t + 8, 1), :].rearrange("p a s -> p (a s)")
                V.tensor_copy(hi, tile_a).then_inc(vector_step, steps.up())
                V.wait_ge(vector_step, steps.now())
                V.tensor_tensor(y_lo[:, bass.ds(t + 8, 1), :].rearrange("p a s -> p (a s)"),
                                         tile_a, hi, ALU.subtract).then_inc(y_tile_ready, y_rdy.up())
                V.wait_ge(y_tile_ready, y_rdy.now())
            V.tensor_copy(small[:, 20:21], rq[:, 0:1]).then_inc(tables_used, 1)
            V.tensor_copy(small[:, 21:22], m[:, 7, 0:1]).then_inc(to_activate, pre.up())
            V.wait_ge(to_activate, pre.now())

            def bank4(j):
                return bank[(j + 2) % 4][:, :]

            def add_product(dst, x, y, chain=True):
                V.tensor_tensor(tile_b, x, y, ALU.mult).then_inc(vector_step, steps.up())
                V.wait_ge(vector_step, steps.now())
                V.tensor_tensor(dst, dst, tile_b, ALU.add).then_inc(vector_step, steps.up())
                V.wait_ge(vector_step, steps.now())

            V.wait_ge(activated, res.due(2))
            for j in range(YA_UNITS):
                arrive(U_YA, j)
                for o in range(2):
                    n = 2 * j + o
                    ins = V.tensor_tensor(m[:, n, :], bank4(n), m[:, n, :], ALU.mult)
                    if o == 0:
                        ins.then_inc(vector_step, steps.up())
                leave(U_YA, j, ins)
            merged = [8, 9, 10, 11, 4, 5, 6, 7]
            for n in range(KD):
                scaled(tile_a, bank4(2 * n), U_YB, 2 * n)
                V.tensor_copy(small[:, 20:21], tile_a[:, 0:1]).then_inc(to_activate, pre.up())
                V.wait_ge(to_activate, pre.now())
                V.wait_ge(activated, res.due())
                arrive(U_YB, 2 * n + 1)
                leave(U_YB, 2 * n + 1, V.tensor_tensor(tile_b, bank4(2 * n + 1), tile_a, ALU.mult))
                V.tensor_tensor(m[:, n, :], m[:, n, :], tile_b, ALU.add)\
                    .then_inc(vector_step, steps.up())
                V.wait_ge(vector_step, steps.now())
                if n < 4:
                    split(merged[n], m[:, n, :])
            for n in range(4, KD):
                split(merged[n], m[:, n, :])
            V.wait_ge(x_landed, 32)

            def residual(u0, j, n, g_col=None):
                arrive(u0, j)
                leave(u0, j, V.tensor_tensor(h[:, n, :], bank4(j), h[:, n, :], ALU.add))
                if g_col is not None:
                    norm_tile(n, g_col, n == KD - 1)

            for n in range(KD):
                residual(U_MIX, n, n, C1_FFN)
            rms()
            V.memset(ssum[:, 0:1], 0.0).then_inc(vector_step, 1)
            steps.k += 1
            u = U_FFN
            tile0 = 0
            for c in FFN_CHUNKS:
                with repeat(V, c // 2, [(steps, 14), (pre, 2), (res, 2), (y_rdy, 2)]) as b:
                    for j in range(2):
                        hidden = b * 2 + (tile0 + j)
                        for gv in range(2):
                            buf, flat = ((ta, tile_a), (tb, tile_b))[gv]
                            scaled(flat, bank4(2 * j + gv), b * 4 + u, 2 * j + gv)
                            dst = (tile_c, tile_d)[gv]
                            cw = [par[:, bass.ds(hidden * 4 + (C1_CONV + gv * FT * 4 + x), 1)] for x in range(4)]
                            V.tensor_scalar(dst, flat, cw[2], cw[3], ALU.mult, ALU.add)\
                                .then_inc(vector_step, steps.up())
                            V.wait_ge(vector_step, steps.now())
                            V.scalar_tensor_tensor(out=dst, in0=buf[:, 15:15 + S], scalar=cw[1], in1=dst,
                                                        op0=ALU.mult, op1=ALU.add)\
                                                            .then_inc(vector_step, steps.up())
                            V.wait_ge(vector_step, steps.now())
                            ins = V.scalar_tensor_tensor(out=dst, in0=buf[:, 14:14 + S], scalar=cw[0],
                                                         in1=dst, op0=ALU.mult, op1=ALU.add)
                            if gv == 0:
                                ins.then_inc(to_activate, pre.up())
                                V.wait_ge(to_activate, pre.now())
                            else:
                                ins.then_inc(vector_step, steps.up())
                                V.wait_ge(vector_step, steps.now())
                        V.wait_ge(activated, res.due())
                        V.tensor_tensor(tile_d, tile_d, tile_c, ALU.mult)\
                            .then_inc(vector_step, steps.up())
                        V.wait_ge(vector_step, steps.now())
                        yt = b * 2 + j
                        hi = y_hi[:, bass.ds(yt, 1), :].rearrange("p a s -> p (a s)")
                        V.tensor_copy(hi, tile_d).then_inc(vector_step, steps.up())
                        V.wait_ge(vector_step, steps.now())
                        V.tensor_tensor(y_lo[:, bass.ds(yt, 1), :].rearrange("p a s -> p (a s)"),
                                                 tile_d, hi, ALU.subtract)\
                                                     .then_inc(y_tile_ready, y_rdy.up())
                        V.wait_ge(y_tile_ready, y_rdy.now())
                u += 2 * c
                tile0 += c
                for n in range(KD):
                    residual(u, n, n)
                u += 8
            for k in range(KD):
                square_tile(k, k == KD - 1)
            rms()
            for k in range(KD):
                ins = V.scalar_tensor_tensor(out=h[:, k, :], in0=h[:, k, :],
                                             scalar=par[:, C1_FIN + k:C1_FIN + k + 1],
                                             in1=rstd[:, :], op0=ALU.mult, op1=ALU.mult)
                if k < KD - 1:
                    ins.then_inc(vector_step, steps.up())
            ins.then_inc(parameters_used, 1)
            V.wait_ge(parameters_used, 1)

            chunk = cst[:, K_CHUNK:K_CHUNK + P]
            with repeat(V, LAYERS, [(steps, N_LAYER), (a_rdy, 24), (y_rdy, 54), (pre, 33), (res, 33),
                                    (root, 15), (sums, 15), (tin, 8), (tout, 4), (rin, 4), (rps, 4),
                                    (score, 16), (mx, 16), (ex, 16), (prb, 16), (pv, 16),
                                    (ofree, 4)]) as layer:
                ul = layer * L_UNITS + U_L
                V.wait_ge(parameters_landed, layer * 16 + 32)
                for e in range(2):
                    l0 = C2_LAM + 128 * e
                    V.tensor_tensor(tile_b[:, 0:64], par[:, l0:l0 + 64], par[:, l0 + 64:l0 + 128], ALU.mult)\
                        .then_inc(vector_step, steps.up())
                    V.wait_ge(vector_step, steps.now())
                    ins = V.tensor_reduce(small[:, 16 + e:17 + e], tile_b[:, 0:64], AX.X, ALU.add)
                    if e == 0:
                        ins.then_inc(vector_step, steps.up())
                        V.wait_ge(vector_step, steps.now())
                ins.then_inc(to_activate, pre.up())
                V.wait_ge(to_activate, pre.now())
                for k in range(KD):
                    norm_tile(k, C2_MIX, k == KD - 1)
                rms()
                V.wait_ge(activated, res.due())
                linit = par[:, C2_LINIT:C2_LINIT + 1]
                V.tensor_scalar(small[:, 18:19], small[:, 17:18], small[:, 16:17], linit,
                                     ALU.subtract, ALU.subtract).then_inc(vector_step, steps.up())
                V.tensor_scalar(small[:, 19:20], linit, -1.0, 1.0, ALU.mult, ALU.add)\
                    .then_inc(vector_step, steps.up())
                V.wait_ge(vector_step, steps.now())
                for j in range(4):
                    scaled(tile_c, bank[j % 2][:, :], ul, j)
                    V.tensor_copy(small[:, 20:21], tile_c[:, 0:1]).then_inc(to_transpose, tin.up())
                    V.wait_ge(to_transpose, tin.now())
                    V.wait_ge(transposed, tout.due())
                    V.tensor_copy(vn[:, j], b_r0[:, :].rearrange("p (a f) -> p a f", f=P))\
                        .then_inc(vector_step, steps.up())
                    V.wait_ge(vector_step, steps.now())
                for j in range(8):
                    scaled(tile_a, bank[j % 2][:, :], ul + L_QK, j)
                    V.tensor_tensor(tile_b, tile_a, tile_a, ALU.mult).then_inc(squares_ready, sums.up())
                    V.wait_ge(squares_ready, sums.now())
                    V.wait_ge(root_ready, root.due())
                    V.reciprocal(tile_b, tile_b).then_inc(vector_step, steps.up())
                    V.wait_ge(vector_step, steps.now())
                    gq = (C2_QG, C2_KG)[j % 2]
                    ins = V.scalar_tensor_tensor(out=(qn, kn)[j % 2][:, j // 2, :], in0=tile_a,
                                                 scalar=par[:, gq:gq + 1], in1=tile_b,
                                                 op0=ALU.mult, op1=ALU.mult)
                    if j % 2:
                        ins.then_inc(retention_input_ready, rin.up())
                        V.wait_ge(retention_input_ready, rin.now())
                    else:
                        ins.then_inc(vector_step, steps.up())

                def head_out(hd):
                    V.wait_ge(root_ready, root.due())
                    V.reciprocal(ssum[:, :], ssum[:, :]).then_inc(vector_step, steps.up())
                    V.wait_ge(vector_step, steps.now())
                    V.scalar_tensor_tensor(out=tile_c, in0=tile_c,
                                                scalar=par[:, C2_SUB:C2_SUB + 1], in1=ssum[:, :],
                                                op0=ALU.mult, op1=ALU.mult)\
                                                    .then_inc(vector_step, steps.up())
                    V.wait_ge(vector_step, steps.now())
                    V.tensor_scalar(tile_c, tile_c, small[:, 19:20], None, ALU.mult)\
                        .then_inc(vector_step, steps.up())
                    V.wait_ge(vector_step, steps.now())
                    split(8 + hd, tile_c)

                for j in range(16):
                    hd, i = j // QT, j % QT
                    n = (i + 1) * P
                    diag = slice(i * P, n)
                    maxima([b_s0[:, 0:n], b_s1[:, 0:n]], 64 ** -0.5, [(b_s0[:, diag], chunk), (b_s1[:, diag], chunk)])
                    V.wait_ge(exp_ready, ex.due())
                    V.reciprocal(small[:, 12:14], small[:, 4:6]).then_inc(vector_step, steps.up())
                    V.wait_ge(vector_step, steps.now())
                    V.tensor_tensor(small[:, 13:14], small[:, 13:14], small[:, 18:19], ALU.mult)\
                        .then_inc(vector_step, steps.up())
                    V.wait_ge(vector_step, steps.now())
                    V.tensor_scalar(prob[:, 1, 0:n], prob[:, 1, 0:n], small[:, 13:14], None, ALU.mult)\
                        .then_inc(vector_step, steps.up())
                    V.wait_ge(vector_step, steps.now())
                    V.scalar_tensor_tensor(out=prob[:, 0, 0:n], in0=prob[:, 0, 0:n],
                                                  scalar=small[:, 12:13], in1=prob[:, 1, 0:n],
                                                  op0=ALU.mult, op1=ALU.add)\
                                                      .then_inc(probs_ready, prb.up())
                    V.wait_ge(probs_ready, prb.now())
                    if 1 <= j <= 4:
                        g = j - 1
                        V.wait_ge(product_ready, rps.due())
                        V.tensor_scalar(tile_a, b_r1[:, :], par[:, C2_PSCALE + g:C2_PSCALE + g + 1],
                                             None, ALU.mult).then_inc(vector_step, steps.up())
                        V.wait_ge(vector_step, steps.now())
                        split(g, tile_a)
                    src = bank[j % 2][:, :]
                    if j < 4:
                        scaled(tile_a, src, ul + L_MIX, j)
                        x, w = ta, 1
                        for lev in range(j + 1):
                            y = (tb, td)[lev % 2]
                            V.tensor_tensor(y[:, 16:], x[:, 16:], x[:, 16 - w:16 - w + S], ALU.add)\
                                .then_inc(vector_step, steps.up())
                            V.wait_ge(vector_step, steps.now())
                            x, w = y, 2 * w
                        y = (tb, td)[(j + 1) % 2]
                        cnt = cst[:, K_CNT + 16 * j:K_CNT + 16 * (j + 1)]
                        V.scalar_tensor_tensor(out=y[:, 16:], in0=x[:, 16:], scalar=1.0 / w, in1=tile_a,
                                                    op0=ALU.mult, op1=ALU.subtract)\
                                                        .then_inc(vector_step, steps.up())
                        V.wait_ge(vector_step, steps.now())
                        V.tensor_tensor(y[:, 16:32], x[:, 16:32], cnt, ALU.mult)\
                            .then_inc(vector_step, steps.up())
                        V.wait_ge(vector_step, steps.now())
                        V.tensor_tensor(y[:, 16:32], y[:, 16:32], ta[:, 16:32], ALU.subtract)\
                            .then_inc(to_transpose, tin.up())
                        V.wait_ge(to_transpose, tin.now())
                    elif j < 12 and j % 2 == 0:
                        scaled(tile_a, src, ul + L_MIX, j)
                    elif j < 12:
                        c = (j - 4) // 2
                        scaled(tile_b, src, ul + L_MIX, j)
                        V.tensor_tensor(tile_d, tile_b, tile_a, ALU.mult)\
                            .then_inc(vector_step, steps.up())
                        V.wait_ge(vector_step, steps.now())
                        cw = [par[:, C2_CONV + 3 * c + x:C2_CONV + 3 * c + x + 1] for x in range(3)]
                        V.tensor_scalar(tile_b, tile_d, cw[2], None, ALU.mult)\
                            .then_inc(vector_step, steps.up())
                        V.wait_ge(vector_step, steps.now())
                        V.scalar_tensor_tensor(out=tile_b, in0=td[:, 15:15 + S], scalar=cw[1], in1=tile_b,
                                                    op0=ALU.mult, op1=ALU.add)\
                                                        .then_inc(vector_step, steps.up())
                        V.wait_ge(vector_step, steps.now())
                        V.scalar_tensor_tensor(out=m[:, c, :], in0=td[:, 14:14 + S], scalar=cw[0], in1=tile_b,
                                                    op0=ALU.mult, op1=ALU.add)\
                                                        .then_inc(vector_step, steps.up())
                        V.wait_ge(vector_step, steps.now())
                    else:
                        c = j - 12
                        scaled(tile_a, src, ul + L_MIX, j)
                        V.tensor_tensor(tile_a, tile_a, m[:, c, :], ALU.mult)\
                            .then_inc(vector_step, steps.up())
                        V.wait_ge(vector_step, steps.now())
                        split(4 + c, tile_a)
                    if i == 0 and j > 0:
                        head_out(hd - 1)
                    if i == 3:
                        V.wait_ge(values_added, pv.due(4))
                        V.tensor_copy(tile_c, b_o[:, :]).then_inc(attention_out_read, ofree.up())
                        V.wait_ge(attention_out_read, ofree.now())
                        V.wait_ge(attention_out_read, ofree.now())
                        V.tensor_tensor(ssum[:, :], tile_c, tile_c, ALU.mult)\
                            .then_inc(squares_ready, sums.up())
                        V.wait_ge(squares_ready, sums.now())
                head_out(3)
                V.memset(m[:, :, :], 0.0).then_inc(vector_step, steps.up())
                V.wait_ge(vector_step, steps.now())
                V.sem_inc(wait_placed, 1)
                with repeat(V, 3, [(steps, 12), (pre, 8), (res, 8)]) as br:
                    ub = ul + L_MERGE + br * 12
                    for half in range(2):
                        for j in range(4):
                            g = work[:, j * S:(j + 1) * S]
                            scaled(g, bank4(j), ub, half * 6 + j)
                            V.tensor_copy(small[:, 20:21], g[:, 0:1]).then_inc(to_activate, pre.up())
                            V.wait_ge(to_activate, pre.now())
                        V.wait_ge(activated, res.due(4))
                        for j in range(2):
                            arrive(ub, half * 6 + 4 + j)
                            for o in range(2):
                                n = 2 * j + o
                                g = work[:, n * S:(n + 1) * S]
                                ins = V.tensor_tensor((tile_a, tile_b)[o], bank4(n), g, ALU.mult)
                                if o == 0:
                                    ins.then_inc(vector_step, steps.up())
                            leave(ub, half * 6 + 4 + j, ins)
                            for o in range(2):
                                n = half * 4 + 2 * j + o
                                V.tensor_tensor(m[:, n, :], m[:, n, :], (tile_a, tile_b)[o], ALU.add)\
                                    .then_inc(vector_step, steps.up())
                                V.wait_ge(vector_step, steps.now())
                for n in range(KD):
                    split(n, m[:, n, :])
                for n in range(KD):
                    residual(ul + L_WO, n, n, C2_MLP)
                rms()
                V.sem_inc(wait_placed, 1)
                with repeat(V, 4, [(steps, 16), (y_rdy, 8)]) as c:
                    uc = ul + L_MLP + c * 16
                    for j in range(8):
                        arrive(uc, j)
                        leave(uc, j, V.scalar_tensor_tensor(out=tile_a, in0=bank4(j), scalar=0.0, in1=rstd[:, :],
                                                            op0=ALU.max, op1=ALU.mult))
                        V.tensor_tensor(tile_a, tile_a, tile_a, ALU.mult)\
                            .then_inc(vector_step, steps.up())
                        V.wait_ge(vector_step, steps.now())
                        split(j, tile_a)
                    for n in range(KD):
                        residual(uc + 8, n, n)
                V.wait_ge(p_landed, layer * 16 + 16)
                for k in range(2):
                    split(8 + k, prob[:, k, :])
                for k in range(KD):
                    norm_tile(k, C2_PLE, k == KD - 1)
                for j in range(4):
                    arrive(ul + L_PLE, j)
                    for o in range(2):
                        ins = V.tensor_copy(m[:, 2 * j + o, :], bank4(2 * j + o))
                        if o == 0:
                            ins.then_inc(vector_step, steps.up())
                    leave(ul + L_PLE, j, ins)
                rms()
                for n in range(KD):
                    scaled(tile_a, bank4(n), ul + L_PLE + 4, n)
                    V.tensor_copy(small[:, 20:21], tile_a[:, 0:1]).then_inc(to_activate, pre.up())
                    V.wait_ge(to_activate, pre.now())
                    V.wait_ge(activated, res.due())
                    V.tensor_tensor(tile_a, tile_a, m[:, n, :], ALU.mult)\
                        .then_inc(vector_step, steps.up())
                    V.wait_ge(vector_step, steps.now())
                    ins = V.tensor_tensor(h[:, n, :], h[:, n, :], tile_a, ALU.add)
                    if n < KD - 1:
                        ins.then_inc(vector_step, steps.up())
                        V.wait_ge(vector_step, steps.now())
                ins.then_inc(parameters_used, 1)
                V.wait_ge(parameters_used, layer + 2)


def _tables():
    f = np.float32
    tok = np.arange(S, dtype=f)

    def angles(half, theta):
        inv = np.power(f(theta), -np.arange(half, dtype=f) / f(half)).astype(f)
        return (tok[None, :] * inv[:, None]).astype(f)

    rope = np.zeros((P, 4, S), f)
    half = ROPE_DIM // 2
    a = angles(half, ROPE_THETA)
    rope[:, 0] = 1.0
    for p in range(P):
        d = p % DH
        if d < 2 * half:
            rope[p, 0] = np.cos(a[d % half])
            rope[p, 1] = np.sin(a[d % half]) * (-1 if d < half else 1)
    a = angles(RDK // 2, RET_THETA)
    for p in range(P):
        d, second = 16 * (p // 32) + p % 16, p % 32 >= 16
        rope[p, 2] = np.cos(a[d])
        rope[p, 3] = np.sin(a[d]) * (1 if second else -1)
    decay = np.zeros((P, RH, S), np.float64)
    dist = np.arange(S)[None, :] - np.arange(P)[:, None]
    for hd in range(RH):
        gamma = 1.0 - 2.0 ** (-5.0 - hd)
        decay[:, hd] = np.where(dist >= 0, gamma ** np.maximum(dist, 0), 0.0) * RDK ** -0.5
    cst = np.zeros((P, K_N), f)
    cst[:, K_ID:K_ID + P] = np.eye(P)
    cst[:, K_ONE:K_ONE + P] = 1.0
    cst[0:64, K_BD:K_BD + 64] = 1.0
    cst[64:, K_BD + 64:K_BD + P] = 1.0
    q, k = np.arange(P)[:, None], np.arange(P)[None, :]
    cst[:, K_CAUSAL:K_CAUSAL + P] = np.where(k <= q, 0.0, NEG)
    cst[:, K_CHUNK:K_CHUNK + P] = np.where(k // 64 <= q // 64, 0.0, NEG)
    for i in range(QT):
        seen = CMP_STRIDE * np.arange(NCMP)[None, :] + CMP_BLOCK - 1 <= i * P + q
        cst[:, K_CMPA + i * NCMP:K_CMPA + (i + 1) * NCMP] = np.where(seen, 0.0, NEG)
        cst[:, K_CMPM + i * NCMP:K_CMPM + (i + 1) * NCMP] = seen
    for g, w in enumerate(POOL_WINDOWS):
        cst[:, K_CNT + 16 * g:K_CNT + 16 * (g + 1)] = 1.0 / np.minimum(np.arange(16) + 1, w)
    return cst, decay.astype(f), rope


def _unit(w, tiles):
    out = np.zeros((P, 8, P), np.float32)
    for at, (k, n) in enumerate(tiles):
        part = w[k * P:(k + 1) * P, n * P:(n + 1) * P]
        out[:, at, :part.shape[1]] = part
    return out.reshape(P, UNIT)


def _full(w, n, k0=0, nk=8):
    return _unit(w, [(k0 + k, n) for k in range(nk)])


def _cols(w, tiles):
    return np.asarray(w).reshape(tiles, P).T


def _stream(x):
    units = []
    w = x["w_in"][0]
    at = np.cumsum([0, 512, 768, 24, 512, 512, 1024, 1024, 2048])
    q_nsa, kv, g_nsa, q_ret, k_ret, v_ret, g_ret, g_m = (w[:, a:b] for a, b in zip(at[:-1], at[1:]))
    heads = q_nsa.reshape(D, HEADS, DH)
    q_nsa = np.concatenate([heads[:, [t, HEADS // 2 + t]].reshape(D, P) for t in range(4)], axis=1)
    perm = np.concatenate([np.r_[16 * j:16 * j + 16, 64 + 16 * j:80 + 16 * j] for j in range(4)])
    perm = np.concatenate([hd * RDK + perm for hd in range(RH)])
    q_ret, k_ret = q_ret[:, perm], k_ret[:, perm]
    units += [_full(kv, n) for n in (0, 1, 3, 5, 2, 4)]
    units += [_full(q_nsa, n) for n in range(4)] + [_full(g_nsa, 0), np.zeros((P, UNIT), np.float32)]
    for w1 in (x["cmp_w1_k"][0], x["cmp_w1_v"][0]):
        units += [_full(w1, n, 8 * half) for n in range(2) for half in range(2)]
    for hd in range(RH):
        units += [_full(q_ret, hd), _full(k_ret, hd), _full(v_ret, 2 * hd), _full(v_ret, 2 * hd + 1)]
        units += [_full(g_m, 2 * hd), _full(g_m, 2 * hd + 1), _full(g_ret, 2 * hd), _full(g_ret, 2 * hd + 1)]

    def two(w, j, nk):
        return _unit(w, [(k, 2 * j + o) for o in range(2) for k in range(nk)])
    rows = x["w_nsa_branch"][0].reshape(HEADS, DH, D)
    w_nsa = np.concatenate([rows[[t, HEADS // 2 + t]].reshape(P, D) for t in range(4)])
    units += [two(w_nsa, j, 4) for j in range(4)]
    for n in range(KD):
        units += [_full(g_m, 8 + n), _full(x["w_ret_branch"][0], n)]
    units += [_full(x["w_mix_out"][0], n) for n in range(KD)]
    up, down, t0 = x["w_ffn_up"][0], x["w_ffn_down"][0], 0
    for c in FFN_CHUNKS:
        for b in range(c):
            units += [_full(up, t0 + b), _full(up, FT + t0 + b)]
        units += [_full(down, n, t0, c) for n in range(KD)]
        t0 += c
    for i in range(LAYERS):
        w = x["w_in_2"][i]
        a, cx, cb, cc, q, k, v = (w[:, 512 * j:512 * (j + 1)] for j in range(7))
        gates = w[:, 3584:]
        units += [_full(v, n) for n in range(4)]
        for n in range(4):
            units += [_full(q, n), _full(k, n)]
        units += [_full(a, n) for n in range(4)]
        for n in range(4):
            units += [_full(cx, n), _full(cc, n)]
        units += [_full(cb, n) for n in range(4)]
        for br, wo in enumerate(("w_pool_out_2", "w_conv_out_2", "w_attn_out_2")):
            for half in range(2):
                units += [_full(gates, br * 8 + half * 4 + n) for n in range(4)]
                units += [two(x[wo][i], half * 2 + j, 4) for j in range(2)]
        units += [_full(x["w_o_2"][i], n) for n in range(KD)]
        for c in range(4):
            units += [_full(x["w_up_2"][i], 8 * c + n) for n in range(KD)]
            units += [_full(x["w_down_2"][i], n, 8 * c) for n in range(KD)]
        units += [two(x["w_ple_proj_2"][i], j, 2) for j in range(4)]
        units += [_full(x["w_ple_gate_2"][i], n) for n in range(KD)]
    assert len(units) == UNITS, (len(units), UNITS)
    both = np.stack(units).reshape(UNITS // 2, 2, P, UNIT)
    return np.ascontiguousarray(both.transpose(0, 2, 1, 3)).reshape(UNITS // 2, P, BLOCK)


def _parameters(x):
    p1 = np.zeros((P, C1_N), np.float32)
    p1[:, C1_MIX:C1_MIX + 8] = _cols(x["norm_mix_w"][0], KD)
    p1[:, C1_FFN:C1_FFN + 8] = _cols(x["norm_ffn_w"][0], KD)
    p1[:, C1_FIN:C1_FIN + 8] = _cols(x["norm_final_w"], KD)
    p1[:, C1_GN:C1_GN + 8] = _cols(x["ret_gn_w"][0], 2 * RH)
    conv = p1[:, C1_CONV:C1_PE].reshape(P, 2 * FT, 4)
    for j in range(3):
        conv[:, :, j] = _cols(x["ffn_conv_w"][0, j], 2 * FT)
    conv[:, :, 3] = _cols(x["ffn_conv_b"][0], 2 * FT)
    for kv, (pe, w2) in enumerate((("cmp_pe_k", "cmp_w2_k"), ("cmp_pe_v", "cmp_w2_v"))):
        p1[:, C1_PE + 16 * kv:C1_PE + 16 * kv + 16] = _cols(x[pe][0], 16)
        p1[:, C1_W2 + 128 * kv:C1_W2 + 128 * (kv + 1)] = x[w2][0].reshape(2, P, DH).transpose(1, 0, 2).reshape(P, P)
    p2 = np.zeros((LAYERS, P, C2_N), np.float32)
    for i in range(LAYERS):
        p = p2[i]
        p[:, C2_MIX:C2_MIX + 8] = _cols(x["norm_mix_g_2"][i], KD)
        p[:, C2_MLP:C2_MLP + 8] = _cols(x["norm_mlp_g_2"][i], KD)
        p[:, C2_PLE:C2_PLE + 8] = _cols(x["norm_ple_g_2"][i], KD)
        p[:, C2_PSCALE:C2_PSCALE + 4] = _cols(x["pool_scale_2"][i], PH)
        conv = p[:, C2_CONV:C2_CONV + 12].reshape(P, 4, 3)
        for j in range(3):
            conv[:, :, j] = _cols(x["conv_w_2"][i, j], 4)
        p[:, C2_QG] = np.tile(x["q_norm_g_2"][i], 2)
        p[:, C2_KG] = np.tile(x["k_norm_g_2"][i], 2)
        p[:, C2_SUB] = x["sub_norm_g_2"][i]
        p[:, C2_LINIT] = 0.8 - 0.6 * np.exp(-0.3 * i)
        for j, name in enumerate(("lam_q1_2", "lam_k1_2", "lam_q2_2", "lam_k2_2")):
            p[:, C2_LAM + 64 * j:C2_LAM + 64 * (j + 1)] = x[name][i][None, :]
        p[:, C2_POOLW:C2_POOLW + PH * P] = x["pool_w_2"][i].transpose(1, 0, 2).reshape(P, PH * P)
    return p1, p2


def _turned(a):
    return np.ascontiguousarray(a.T.reshape(-1, P, S).transpose(1, 0, 2))


def kernel(**inputs):
    import concourse.bacc as bacc
    from concourse.bass_utils import run_bass_kernel_spmd

    x = {name: np.asarray(a) for name, a in inputs.items()}
    cst, decay, rope = _tables()
    par1, par2 = _parameters(x)
    arrays = {
        "stream": _stream(x), "xT": _turned(x["x"][0]), "tab": cst, "decay": decay, "rope": rope,
        "par1": par1, "par2": par2, "pT": np.stack([_turned(p[0]) for p in x["p_2"]]),
    }
    nc = bacc.Bacc("TRN2", target_bir_lowering=False, num_devices=1)
    args = [nc.dram_tensor(name, a.shape, F32, kind="ExternalInput").ap() for name, a in arrays.items()]
    out = nc.dram_tensor("outT", (P, KD, S), F32, kind="ExternalOutput").ap()
    build(nc, *args, out)
    r = run_bass_kernel_spmd(nc, [arrays], core_ids=[0])
    got = np.asarray(r.results[0]["outT"])
    return np.ascontiguousarray(got.transpose(1, 0, 2).reshape(D, S).T).reshape(1, S, D)
```

```python
from contextlib import ExitStack, contextmanager

import numpy as np

import concourse.bass as bass
from concourse import mybir

F32 = mybir.dt.float32
F32R = mybir.dt.float32r
ALU = mybir.AluOpType
ACT = mybir.ActivationFunctionType
AX = mybir.AxisListType

P = 128
S = 512
QT = S // P
D = 1024
KD = D // P
NEG = -1e30
EPS = 1e-6
UNIT = 8 * P
BLOCK = 2 * UNIT

HEADS, KVG, DH = 8, 2, 64
CMP_BLOCK, CMP_STRIDE, CMP_HIDDEN = 32, 16, 256
NCMP = (S - CMP_BLOCK) // CMP_STRIDE + 1
ROPE_DIM, ROPE_THETA = DH // 4, 500000.0
RH, RDK, RDV, RET_THETA = 4, 128, 256, 10000.0
DFF = 2816
FT = DFF // P
LAYERS = 2
PH = 4
POOL_WINDOWS = (2, 4, 8, 16)
DFF2 = 4096
PLE = 256

NSA_UNITS = 12
CMP_UNITS = 8
RET_UNITS = 8
YA_UNITS = 4
YB_UNITS = 16
MIX_UNITS = 8
FFN_CHUNKS = (8, 8, 6)
U_CMP = NSA_UNITS
U_RET = U_CMP + CMP_UNITS
U_YA = U_RET + RH * RET_UNITS
U_YB = U_YA + YA_UNITS
U_MIX = U_YB + YB_UNITS
U_FFN = U_MIX + MIX_UNITS
U_L = U_FFN + sum(2 * c + 8 for c in FFN_CHUNKS)
L_QK, L_MIX, L_MERGE = 4, 12, 28
L_WO = L_MERGE + 36
L_MLP = L_WO + 8
L_PLE = L_MLP + 64
L_UNITS = L_PLE + 12
UNITS = U_L + LAYERS * L_UNITS
GROUPS = UNITS // 4

C1_MIX, C1_FFN, C1_FIN, C1_GN = 0, 8, 16, 24
C1_CONV = 32
C1_PE = C1_CONV + 2 * FT * 4
C1_W2 = C1_PE + 32
C1_N = C1_W2 + 256
C2_MIX, C2_MLP, C2_PLE = 0, 8, 16
C2_PSCALE, C2_CONV, C2_QG, C2_KG, C2_SUB, C2_LINIT = 24, 28, 40, 41, 42, 43
C2_LAM = 48
C2_POOLW = C2_LAM + 256
C2_N = C2_POOLW + PH * P
PAR_N = max(C1_N, C2_N)

K_ID, K_ONE, K_BD, K_CAUSAL, K_CHUNK = 0, 128, 256, 384, 512
K_CMPA = 640
K_CMPM = K_CMPA + QT * NCMP
K_CNT = K_CMPM + QT * NCMP
K_N = K_CNT + PH * 16
N_RET, N_LAYER = 80, 308
POOLED = [1, 0, 1, 0]
SWAP_NSA = [i + 8 if i < 8 else i - 8 if i < 16 else i for i in range(32)]
SWAP_RET = [(i + 16) % 32 for i in range(32)]


class Count:

    def __init__(self, start=0):
        self.base, self.k = start, 0

    def now(self):
        return self.base + self.k

    def due(self, n=1):
        self.k += n
        return self.now()

    def up(self, n=1):
        self.k += n
        return n


@contextmanager
def repeat(eng, n, rises):
    start = [(t.base, t.k) for t, _ in rises]
    with eng.Fori(0, n) as i:
        for (t, rise), (base, k) in zip(rises, start):
            t.base, t.k = base + i * rise + k, 0
        yield i
        for m, (t, rise) in enumerate(rises):
            assert t.k == rise, (f"count {m} of the loop", t.k, rise)
    for (t, rise), (base, k) in zip(rises, start):
        t.base, t.k = base, k + n * rise


def build(nc, stream, xT, tab, decay, rope, par1, par2, pT, out):
    ctx = ExitStack()
    with ctx:
        def sb(name, shape, dt=F32):
            return ctx.enter_context(nc.sbuf_tensor(name, shape, dt))

        def sem(name):
            return ctx.enter_context(nc.semaphore(name))

        bank = [ctx.enter_context(nc.psum_tensor(f"bank{i}", [P, S], F32)) for i in range(2)]
        both = ctx.enter_context(nc.psum_tensor("both", [P, 2 * S], F32))
        bank += [both[:, 0:S], both[:, S:2 * S]]
        bank += [ctx.enter_context(nc.psum_tensor(f"bank{i}", [P, S], F32)) for i in range(4, 8)]
        scores = both[:, :].rearrange("p (e s) -> p e s", e=2)
        b_s0, b_s1, b_cmp, b_o, b_r0, b_r1 = bank[2:8]

        raw = sb("raw", [P, 2, BLOCK])
        w_hi = sb("w_hi", [P, 2, BLOCK], F32R)
        w_lo = sb("w_lo", [P, 2, BLOCK], F32R)
        a_hi = sb("a_hi", [P, KD, S], F32R)
        a_lo = sb("a_lo", [P, KD, S], F32R)
        y_hi = sb("y_hi", [P, 12, S], F32R)
        y_lo = sb("y_lo", [P, 12, S], F32R)
        h = sb("h", [P, KD, S])
        m = sb("m", [P, KD, S])
        par = sb("par", [P, PAR_N])
        cst = sb("cst", [P, K_N])
        rstd = sb("rstd", [P, S])
        ssum = sb("ssum", [P, S])
        ta = sb("ta", [P, 16 + S])
        tb = sb("tb", [P, 16 + S])
        td = sb("td", [P, 16 + S])
        tile_c = sb("tile_c", [P, S])[:, :]
        prob = sb("prob", [P, 2, S])
        pt = sb("pt", [P, 2, S])
        small = sb("small", [P, 64])
        mix_gain = sb("mix_gain", [P, LAYERS * KD])
        work = sb("work", [P, 9 * S + 288])

        ident = cst[:, K_ID:K_ID + P]
        ones = cst[:, K_ONE:K_ONE + P]
        ones2 = cst[:, K_BD:K_BD + P]
        tile_a, tile_b, tile_d = ta[:, 16:], tb[:, 16:], td[:, 16:]
        eps = small[:, 60:61]
        decay_t = h[:, 0:4, :]
        rope_cn, rope_sn, rope_cr, rope_sr = (h[:, 4 + i, :] for i in range(4))

        def w1(at, n):
            return work[:, at:at + n]
        ks, kw = w1(0, S), w1(S, S)
        vs, vw = (w1((2 + i) * S, S).rearrange("p (a f) -> p a f", f=P) for i in range(2))
        rv = w1(4 * S, 2 * S).rearrange("p (a f) -> p a f", f=RDV)
        rp = w1(6 * S, 1280)
        rg = rp[:, 0:2 * S].rearrange("p (e s) -> p e s", e=2)
        at = 6 * S + 1280
        kc = w1(at, 32)
        vc = w1(at + 32, P)
        gn = w1(at + 160, QT * 24).rearrange("p (i c) -> p i c", c=24)
        gates = small[:, 28:52].rearrange("p (i c) -> p i c", c=6)
        hid = w1(at + 256, 128).rearrange("p (k c) -> p k c", c=64)
        hidden_rows = (tile_c, tile_b)
        pc = w1(at + 384, 32)
        ptc = w1(at + 416, P)
        rq, rk = h[:, 4, :], h[:, 5, :]
        qt = tile_d
        xc_hi = [y_hi[:, 2 * i:2 * i + 2, :].rearrange("p a s -> p (a s)")[:, 0:992]
                 .rearrange("p (m g c) -> p m g c", g=2, c=NCMP) for i in range(2)]
        xc_lo = [y_lo[:, 2 * i:2 * i + 2, :].rearrange("p a s -> p (a s)")[:, 0:992]
                 .rearrange("p (m g c) -> p m g c", g=2, c=NCMP) for i in range(2)]
        xc = rp[:, 0:992].rearrange("p (m g c) -> p m g c", g=2, c=NCMP)
        qn = w1(0, 4 * S).rearrange("p (h s) -> p h s", s=S)
        kn = w1(4 * S, 4 * S).rearrange("p (h s) -> p h s", s=S)
        vn = m[:, 4:8, :].rearrange("p h (a f) -> p h a f", f=P)

        first_unit_landed = sem("first_unit_landed")
        landed = [sem("block_landed_0"), sem("block_landed_1")]
        hi_done = sem("unit_hi_done")
        lo_done = sem("unit_lo_done")
        unit_done = sem("unit_done")
        evac = sem("unit_evacuated")
        x_tile_landed = [sem(f"x_tile_landed_{k}") for k in range(KD)]
        x_landed = sem("x_landed")
        ones_landed = sem("ones_landed")
        first_gain_landed = sem("first_gain_landed")
        constants_landed = sem("constants_landed")
        tables_landed = sem("tables_landed")
        gains_landed = sem("gains_landed")
        h_tile_ready = sem("h_tile_ready")
        hi_tile_ready = sem("hi_tile_ready")
        x_square_ready = sem("x_square_ready")
        squares_added = sem("squares_added")
        parameters_landed = sem("parameters_landed")
        p_landed = sem("p_landed")
        x_used = sem("x_used")
        tables_used = sem("tables_used")
        parameters_used = sem("parameters_used")
        a_tile_ready = sem("a_tile_ready")
        y_tile_ready = sem("y_tile_ready")
        squares_ready = sem("squares_ready")
        square_sum_done = sem("square_sum_done")
        root_ready = sem("root_ready")
        activated = sem("activated")
        to_activate = sem("to_activate")
        to_transpose = sem("to_transpose")
        transposed = sem("transposed")
        gelu_ready = sem("gelu_ready")
        root_inverted = sem("root_inverted")
        output_gated = sem("output_gated")
        output_scaled = sem("output_scaled")
        output_rounded = sem("output_rounded")
        hidden_ready = sem("hidden_ready")
        compressed = sem("compressed")
        scores_ready = sem("scores_ready")
        max_ready = sem("max_ready")
        exp_ready = sem("exp_ready")
        probs_ready = sem("probs_ready")
        probs_transposed = sem("probs_transposed")
        probs_copied = sem("probs_copied")
        values_added = sem("values_added")
        attention_out_read = sem("attention_out_read")
        retention_input_ready = sem("retention_input_ready")
        product_ready = sem("product_ready")
        product_read = sem("product_read")
        vector_step = sem("vector_step")
        out_stored = sem("out_stored")
        table_loaded = sem("table_loaded")
        wait_placed = sem("wait_placed")

        block = ctx.enter_context(nc.Block())

        def unit_slot(j):
            return (j // 2) % 2, slice((j % 2) * UNIT, (j % 2 + 1) * UNIT)

        @block.sync
        def _(sp):
            sp.dma_start(par[:, 0:C1_FFN], par1[:, 0:C1_FFN]).then_inc(first_gain_landed, 16)
            for k in range(KD):
                sp.dma_start(h[:, k, :], xT[:, k, :]).then_inc(x_tile_landed[k], 16)
            sp.dma_start(raw[:, 0, UNIT:], stream[0, :, UNIT:]).then_inc(landed[0], 16)
            sp.dma_start(raw[:, 1], stream[1]).then_inc(landed[1], 16)
            with sp.Fori(1, GROUPS) as g:
                for s in range(2):
                    sp.wait_ge(lo_done, g * 4 - 2 + 2 * s)
                    sp.dma_start(raw[:, s], stream[g * 2 + s]).then_inc(landed[s], 16)
            for s in range(2):
                sp.wait_ge(lo_done, GROUPS * 4 - 2 + 2 * s)
                sp.dma_start(raw[:, s], stream[s]).then_inc(landed[s], 16)
            for s in range(2):
                sp.wait_ge(landed[s], 16 * (GROUPS + 1))
            for n in range(KD):
                sp.wait_ge(h_tile_ready, KD * LAYERS + n + 1)
                sp.dma_start(out[:, n, :], h[:, n, :]).then_inc(out_stored, 16)
            sp.wait_ge(out_stored, 16 * KD)

        @block.gpsimd
        def _(pool):
            def lo_part(u, j):
                s, cols = unit_slot(j)
                pool.wait_ge(hi_done, u + 1)
                pool.tensor_tensor(w_lo[:, s, cols], raw[:, s, cols], w_hi[:, s, cols],
                                   ALU.subtract).then_inc(lo_done, 1)

            with pool.Fori(0, U_RET // 4) as g:
                for j in range(4):
                    lo_part(g * 4 + j, j)
            for j in range(3):
                lo_part(U_RET + j, j)
            with pool.Fori(0, RH) as t:
                for j in range(3, RET_UNITS + 3):
                    lo_part(t * RET_UNITS + U_RET + j, j % 4)
                pool.wait_ge(activated, t + 2)
                pool.wait_ge(squares_ready, t + 1)
                pool.tensor_tensor(rg[:, 0, :], rg[:, 0, :], rq, ALU.mult).then_inc(output_gated, 1)
                pool.tensor_tensor(rg[:, 1, :], rg[:, 1, :], rk, ALU.mult).then_inc(output_gated, 1)
                pool.wait_ge(output_gated, t * 2 + 2)
                pool.tensor_tensor(rg, rg, small[:, 24:26].unsqueeze(2).to_broadcast([P, 2, S]), ALU.mult)\
                    .then_inc(output_scaled, 1)
                pool.wait_ge(output_scaled, t * 3 + 1)
                pool.wait_ge(root_inverted, t + 1)
                for e in range(2):
                    pool.tensor_tensor(rg[:, e, :], rg[:, e, :], tile_c, ALU.mult)\
                        .then_inc(output_scaled, 1)
                pool.wait_ge(output_scaled, t * 3 + 3)
                hi, lo = (y[:, bass.ds(t * 2, 2), :] for y in (y_hi, y_lo))
                pool.tensor_copy(hi, rg).then_inc(output_rounded, 1)
                pool.wait_ge(output_rounded, t + 1)
                pool.tensor_tensor(lo, rg, hi, ALU.subtract).then_inc(y_tile_ready, 2)
            lo_part(U_YA + 3, 3)
            with pool.Fori(U_YA // 4 + 1, U_L // 4) as g:
                for j in range(4):
                    lo_part(g * 4 + j, j)
            with pool.Fori(0, LAYERS) as layer:
                ul = layer * L_UNITS + U_L
                for j in range(3):
                    lo_part(ul + j, j)
                for k in range(1, KD):
                    pool.wait_ge(x_square_ready, layer * KD + (KD + k + 1))
                    if k > 1:
                        pool.wait_ge(squares_added, layer * (KD - 2) + (k - 1))
                    ins = pool.tensor_tensor(ssum[:, :], m[:, 0, :] if k == 1 else ssum[:, :], m[:, k, :], ALU.add)
                    if k < KD - 1:
                        ins.then_inc(squares_added, 1)
                ins.then_inc(squares_ready, 1)
                lo_part(ul + 3, 3)
                with pool.Fori(1, L_UNITS // 4) as g:
                    for j in range(4):
                        lo_part(ul + g * 4 + j, j)
            for j in range(3):
                lo_part(GROUPS * 4 + j, j)

        @block.scalar
        def _(act):
            def hi_part(u0, j):
                g4 = u0 + (j // 4) * 4
                j %= 4
                s, cols = unit_slot(j)
                if j % 2 == 0:
                    act.wait_ge(landed[s], g4 * 4 + 16)
                act.wait_ge(unit_done, g4 + (j + 1))
                act.activation(w_hi[:, s, cols], raw[:, s, cols], ACT.Copy).then_inc(hi_done, 1)

            def ahead(u0, j):
                hi_part(u0, j + 3)

            pre, res = Count(), Count()
            tables = Count(1)
            sump, root = Count(), Count()
            mx, ex = Count(), Count()
            gelu = Count()
            ptp, ptr, pv = Count(), Count(), Count()

            def load_table(func):
                act.wait_ge(table_loaded, tables.now())
                act.activation(small[:, 54:55], small[:, 55:56], func)\
                    .then_inc(table_loaded, tables.up())

            def tile_root(dst, src, scale, load=True):
                if load:
                    load_table(ACT.Sqrt)
                act.wait_ge(square_sum_done, sump.due())
                act.activation(dst, src, ACT.Sqrt, bias=eps, scale=scale)\
                    .then_inc(root_ready, root.up())

            def square(k):
                act.activation(m[:, k, :], h[:, k, :], ACT.Square).then_inc(x_square_ready, 1)

            act.dma_start(raw[:, 0, 0:UNIT], stream[0, :, 0:UNIT]).then_inc(first_unit_landed, 16)
            act.dma_start(cst[:, K_ONE:K_BD], tab[:, K_ONE:K_BD]).then_inc(ones_landed, 16)
            act.wait_ge(first_unit_landed, 16)
            act.activation(w_hi[:, 0, 0:UNIT], raw[:, 0, 0:UNIT], ACT.Copy).then_inc(hi_done, 1)
            for k in range(KD):
                act.wait_ge(x_tile_landed[k], 16)
                square(k)
            act.wait_ge(landed[0], 16)
            hi_part(0, 1)
            act.dma_start(par[:, C1_FFN:C1_N], par1[:, C1_FFN:C1_N]).then_inc(parameters_landed, 16)
            act.dma_start(cst[:, 0:K_ONE], tab[:, 0:K_ONE]).then_inc(constants_landed, 16)
            act.dma_start(cst[:, K_BD:], tab[:, K_BD:]).then_inc(constants_landed, 16)
            for i in range(LAYERS):
                act.dma_start(mix_gain[:, i * KD:(i + 1) * KD], par2[i, :, C2_MIX:C2_MIX + KD])\
                    .then_inc(gains_landed, 16)
            hi_part(0, 2)
            act.wait_ge(to_activate, pre.due())
            act.sem_inc(table_loaded, 1)
            act.wait_ge(x_used, 1)
            act.dma_start(h[:, 0:4, :], decay).then_inc(tables_landed, 16)
            act.dma_start(h[:, 4:8, :], rope).then_inc(tables_landed, 16)
            tile_root(rstd[:, :], b_r1[:, :], 1.0 / D)

            def run(u0, n):
                for j in range(n):
                    ahead(u0, j)

            run(0, NSA_UNITS)
            act.wait_ge(to_activate, pre.due())
            act.activation(gn, gn, ACT.Sigmoid).then_inc(activated, res.up())
            for j in range(CMP_UNITS):
                if j in (4, 7):
                    load_table(ACT.Gelu_apprx_tanh)
                    kv = j // 6
                    act.wait_ge(evac, U_CMP + kv * 4 + 8)
                    act.activation(hidden_rows[kv][0:KVG * NCMP, 0:CMP_HIDDEN],
                                   hidden_rows[kv][0:KVG * NCMP, 0:CMP_HIDDEN], ACT.Gelu_apprx_tanh)\
                        .then_inc(gelu_ready, gelu.up())
                ahead(U_CMP, j)
            load_table(ACT.Exp)

            def softmax_step(parts, last_scale):
                act.wait_ge(max_ready, mx.due())
                for n, (dst, src, b) in enumerate(parts):
                    ins = act.activation(dst, src, ACT.Exp, bias=small[:, b:b + 1], scale=last_scale,
                                         accum_out=small[:, b + 4:b + 5])
                ins.then_inc(exp_ready, ex.up())

            def copy_transposed(parts):
                act.wait_ge(values_added, pv.due())
                act.wait_ge(probs_transposed, ptp.due())
                for dst, src in parts:
                    ins = act.activation(dst, src, ACT.Copy)
                ins.then_inc(probs_copied, ptr.up())

            with repeat(act, RH, [(res, 1), (mx, 8), (ex, 8), (ptp, 8), (ptr, 8), (pv, 8),
                                  (sump, 1), (root, 1), (tables, 2)]) as t:
                u0 = t * RET_UNITS + U_RET
                for j in range(RET_UNITS):
                    i = j % QT
                    n = (i + 1) * P
                    softmax_step([(pc[:, 0:NCMP], b_cmp[:, 0:NCMP], 0),
                                  (prob[:, 0, 0:n], b_s0[:, 0:n], 1),
                                  (prob[:, 1, 0:n], b_s1[:, 0:n], 2)], DH ** -0.5)
                    ahead(u0, j)
                    if j == 7:
                        act.wait_ge(evac, u0 + 11)
                        act.activation(rg, rg, ACT.Silu).then_inc(activated, res.up())
                    copy_transposed([(pt[:, :, 0:n], scores[:, :, 0:n]),
                                     (ptc[0:NCMP, :], b_cmp[0:NCMP, 0:P])])
                    if j == 7:
                        tile_root(tile_c, b_r1[:, :], 1.0 / RDV)
                        load_table(ACT.Exp)
            act.wait_ge(tables_used, 1)
            act.dma_start(h[:, :, :], xT).then_inc(x_landed, 16)
            act.wait_ge(to_activate, pre.due())
            for half in range(2):
                act.activation(m[:, 4 * half:4 * half + 4, :], m[:, 4 * half:4 * half + 4, :],
                                      ACT.Sigmoid).then_inc(activated, res.up())
            run(U_YA, YA_UNITS)
            for j in range(YB_UNITS):
                ahead(U_YB, j)
                if j % 2 == 0:
                    act.wait_ge(evac, U_YB + j + 5)
                    act.activation(tile_a, tile_a, ACT.Sigmoid).then_inc(activated, res.up())
            run(U_MIX, MIX_UNITS)
            tile_root(rstd[:, :], b_r1[:, :], 1.0 / D)
            u = U_FFN
            for c in FFN_CHUNKS:
                with repeat(act, c // 2, [(pre, 2), (res, 2)]) as b:
                    for j in range(4):
                        ahead(b * 4 + u, j)
                        if j % 2 == 1:
                            act.wait_ge(to_activate, pre.due())
                            act.activation(tile_c, tile_c, ACT.Silu).then_inc(activated, res.up())
                u += 2 * c
                run(u, 8)
                u += 8
            tile_root(rstd[:, :], b_r1[:, :], 1.0 / D)
            hready = Count()
            load_table(ACT.Copy)

            with repeat(act, LAYERS, [(pre, 1), (res, 33), (mx, 16), (ex, 16), (ptp, 16), (ptr, 16),
                                      (pv, 16), (sump, 15), (root, 15), (hready, KD),
                                      (tables, 21)]) as layer:
                ul = layer * L_UNITS + U_L
                act.wait_ge(unit_done, ul + 4)
                for k in range(KD):
                    act.wait_ge(h_tile_ready, hready.due())
                    act.activation(a_hi[:, k, :], h[:, k, :], ACT.Copy,
                                   scale=mix_gain[:, bass.ds(layer * KD + k, 1)])\
                        .then_inc(hi_tile_ready, 1)
                for k in range(KD):
                    square(k)
                act.wait_ge(parameters_used, layer + 1)
                act.dma_start(par[:, 0:C2_N], par2[layer]).then_inc(parameters_landed, 16)
                ahead(ul, 0)
                tile_root(rstd[:, :], b_r1[:, :], 1.0 / D)
                lam = small[:, 16:18]
                act.wait_ge(to_activate, pre.due())
                act.activation(lam, lam, ACT.Exp).then_inc(activated, res.up())
                ul = layer * L_UNITS + U_L
                for j in range(1, 4):
                    ahead(ul, j)
                def attention_step(s):
                    n = (s % QT + 1) * P
                    softmax_step([(prob[:, e, 0:n], (b_s0, b_s1)[e][:, 0:n], e) for e in range(2)],
                                 64 ** -0.5)

                def attention_copy(s):
                    n = (s % QT + 1) * P
                    copy_transposed([(pt[:, 0, 0:n], b_cmp[:, 0:n])])

                for j in range(8):
                    if j == 7:
                        load_table(ACT.Exp)
                        attention_step(0)
                    ahead(ul + L_QK, j)
                    if j > 0:
                        tile_root((tile_b, tile_c)[(j - 1) % 2], (b_r0, b_r1)[(j - 1) % 2][:, :], 1.0 / 64)
                load_table(ACT.Exp)
                attention_copy(0)
                for k in range(16):
                    if k < 15:
                        attention_step(k + 1)
                    ahead(ul + L_MIX, k)
                    if k == 0:
                        tile_root(tile_c, b_r1[:, :], 1.0 / 64)
                        load_table(ACT.Exp)
                    if k > 0 and k % QT == 0 or k == 15:
                        tile_root(ssum[:, :], b_r0[:, :], 1.0 / P)
                        if k < 15:
                            load_table(ACT.Exp)
                    if k < 15:
                        attention_copy(k + 1)
                act.dma_start(prob[:, :, :], pT[layer]).then_inc(p_landed, 16)
                with repeat(act, 3, [(res, 8)]) as br:
                    for half in range(2):
                        for j in range(6):
                            ub = ul + L_MERGE + br * 12
                            ahead(ub, half * 6 + j)
                            if j < 4:
                                act.wait_ge(evac, ub + (half * 6 + j + 5))
                                g = work[:, j * S:(j + 1) * S]
                                act.activation(g, g, ACT.Sigmoid).then_inc(activated, res.up())
                run(ul + L_WO, 8)
                tile_root(rstd[:, :], b_r1[:, :], 1.0 / D)
                with repeat(act, 4, []) as c:
                    run(ul + L_MLP + c * 16, 16)
                for j in range(12):
                    ahead(ul + L_PLE, j)
                    if j == 1:
                        tile_root(rstd[:, :], b_r1[:, :], 1.0 / D)
                    if j >= 4:
                        act.wait_ge(evac, ul + (L_PLE + j + 5))
                        g = (tile_a, tile_b)[j % 2]
                        act.activation(g, g, ACT.Sigmoid).then_inc(activated, res.up())

        @block.tensor
        def _(pe):
            pe.sem_inc(unit_done, 4)
            pe.sem_inc(values_added, 1)
            a_rdy, y_rdy = Count(), Count()
            sums, sump = Count(), Count()
            tin, tout = Count(), Count()
            cx, cp = Count(), Count()
            score, prb, ptp, ptr, pv = (Count() for _ in range(5))
            ofree = Count()
            rin, rps, rfree = Count(), Count(), Count()

            def product(dst, w, rhs_hi, rhs_lo, nk, first=None, start=True, stop=True):
                s, c0 = w
                for k in range(nk):
                    if first is not None:
                        first(k)
                    cols = slice(c0 + k * P, c0 + (k + 1) * P)
                    pe.matmul(dst, w_hi[:, s, cols], rhs_hi(k), start=start and k == 0, stop=False)
                    pe.matmul(dst, w_hi[:, s, cols], rhs_lo(k), start=False, stop=False)
                    ins = pe.matmul(dst, w_lo[:, s, cols], rhs_hi(k), start=False,
                                    stop=stop and k == nk - 1)
                return ins

            def unit(u0, j, lag, dsts, rhs, nk, first=None, start=True, stop=True):
                s, cols = unit_slot(j)
                pe.wait_ge(lo_done, u0 + (j + 1))
                pe.wait_ge(evac, u0 + (j + 5 - lag))
                hi, lo = rhs
                for o, dst in enumerate(dsts):
                    ins = product(dst, (s, cols.start + o * nk * P), hi, lo, nk,
                                  first if o == 0 else None, start, stop)
                ins.then_inc(unit_done, 1)

            def a_op(n=S):
                return (lambda k: a_hi[:, k, :]), (lambda k: a_lo[:, k, :])

            def y_op(at=0):
                return (lambda k: y_hi[:, at + k, :]), (lambda k: y_lo[:, at + k, :])

            def next_a(k):
                pe.wait_ge(a_tile_ready, a_rdy.due())

            def next_y(k):
                pe.wait_ge(y_tile_ready, y_rdy.due())

            def square_sum(dst=None, w=None, src=None):
                pe.wait_ge(squares_ready, sums.due())
                pe.matmul((b_r1 if dst is None else dst)[:, :], ones if w is None else w,
                                  ssum[:, :] if src is None else src, start=True, stop=True)\
                                      .then_inc(square_sum_done, sump.up())

            pe.wait_ge(ones_landed, 16)
            def bank4(j):
                return bank[(j + 2) % 4][:, :]

            def result_transposes(u0, j, dst, src):
                pe.wait_ge(evac, u0 + (j + 5))
                for i in range(QT):
                    ins = pe.transpose(dst[:, i * P:(i + 1) * P], src[:, i * P:(i + 1) * P], ident)
                ins.then_inc(transposed, tout.up())

            def x_tile(k):
                if k > 0:
                    pe.wait_ge(x_square_ready, k)
                    pe.matmul(b_r1[:, :], ones, m[:, k - 1, :], start=k == 1, stop=False,
                              skip_group_check=True)
                next_a(k)

            for j in range(NSA_UNITS):
                unit(0, j, 4, [bank4(j)], a_op(), 8 if j < 11 else 1, x_tile if j == 0 else None)
                if j == 0:
                    pe.wait_ge(x_square_ready, KD)
                    pe.matmul(b_r1[:, :], ones, m[:, KD - 1, :], start=False, stop=True,
                              skip_group_check=True).then_inc(square_sum_done, sump.up())
                if j == 3:
                    pe.wait_ge(constants_landed, 32)
                    result_transposes(0, 2, b_r0, prob[:, 0, :])
                if j == 4:
                    result_transposes(0, 3, b_cmp, prob[:, 1, :])
            result_transposes(0, 10, b_r0, prob[:, 0, :])
            def hidden_unit(kv, q):
                j = kv * 4 + q
                s, cols = unit_slot(j)
                pe.wait_ge(lo_done, U_CMP + j + 1)
                if q == 0:
                    pe.wait_ge(evac, U_CMP + 3 + kv)
                dst = bank[kv][0:KVG * NCMP, 0:CMP_HIDDEN]
                for k in range(4):
                    w = slice(cols.start + k * CMP_HIDDEN, cols.start + (k + 1) * CMP_HIDDEN)
                    x_hi, x_lo = (x[kv][:, 4 * q + k].rearrange("p g c -> p (g c)") for x in (xc_hi, xc_lo))
                    pe.matmul(dst, x_hi, w_hi[:, s, w], start=q == 0 and k == 0, stop=False)
                    pe.matmul(dst, x_lo, w_hi[:, s, w], start=False, stop=False)
                    ins = pe.matmul(dst, x_hi, w_lo[:, s, w], start=False, stop=q == 3 and k == 3)
                ins.then_inc(unit_done, 1)

            def hidden_transposes(kv):
                pe.wait_ge(gelu_ready, cx.due())
                for k in range(2):
                    ins = pe.transpose(b_cmp[:, k * 64:k * 64 + KVG * NCMP],
                                       hidden_rows[kv][0:KVG * NCMP, k * P:(k + 1) * P],
                                       ident[0:KVG * NCMP, 0:KVG * NCMP])
                ins.then_inc(transposed, tout.up())

            def compress(kv):
                pe.wait_ge(hidden_ready, kv + 1)
                w2 = par[:, C1_W2 + kv * 128:C1_W2 + (kv + 1) * 128].rearrange("p (k d) -> p k d", d=DH)
                for g in range(KVG):
                    for k in range(2):
                        hc = hid[:, k, g * NCMP:(g + 1) * NCMP]
                        if kv == 0:
                            ins = pe.matmul(b_r0[g * DH:(g + 1) * DH, 0:NCMP], w2[:, k, :], hc,
                                            start=k == 0, stop=k == 1)
                        else:
                            ins = pe.matmul(b_r1[0:NCMP, g * DH:(g + 1) * DH], hc, w2[:, k, :],
                                            start=k == 0, stop=k == 1)
                ins.then_inc(compressed, cp.up())

            pe.wait_ge(y_tile_ready, y_rdy.due())
            for q in range(4):
                hidden_unit(0, q)
            pe.wait_ge(y_tile_ready, y_rdy.due())
            for q in range(4):
                hidden_unit(1, q)
                if q == 1:
                    hidden_transposes(0)
            compress(0)
            hidden_transposes(1)
            compress(1)

            with repeat(pe, RH, [(score, 8), (prb, 8), (ptp, 8), (ptr, 8), (pv, 8), (ofree, 1),
                                 (rin, 4), (rps, 9), (rfree, 8), (sums, 1), (sump, 1),
                                 (tin, 1)]) as t:
                u0 = t * RET_UNITS + U_RET
                pe.wait_ge(to_transpose, tin.due())

                def ret_scores(a, dst):
                    pe.matmul(dst[:, 0:S - a * P], rk[:, a * P:(a + 1) * P], rq[:, a * P:S],
                                     start=True, stop=True).then_inc(product_ready, rps.up())

                def ret_transposes(dst, src):
                    pe.wait_ge(retention_input_ready, rin.due())
                    for a in range(QT):
                        ins = pe.transpose(dst[:, a * P:(a + 1) * P], src[:, a * P:(a + 1) * P], ident)
                    ins.then_inc(product_ready, rps.up())

                def ret_values(e, dst):
                    at = 0
                    for a in range(QT):
                        n = S - a * P
                        ins = pe.matmul(dst[:, a * P:S], rv[:, a, e * P:(e + 1) * P], rp[:, at:at + n],
                                        start=a == 0, stop=a == QT - 1, skip_group_check=True)
                        at += n
                    ins.then_inc(product_ready, rps.up())

                def attention_scores(j):
                    g, i = j // QT, j % QT
                    n = (i + 1) * P
                    rows = slice(g * DH, (g + 1) * DH)
                    q = qt[rows, i * P:(i + 1) * P]
                    pe.matmul(b_cmp[:, 0:NCMP], q, kc[rows, 0:NCMP], start=True, stop=True)
                    pe.matmul(b_s0[:, 0:n], q, ks[rows, 0:n], start=True, stop=True)
                    pe.matmul(b_s1[:, 0:n], q, kw[rows, 0:n], start=True, stop=True)\
                        .then_inc(scores_ready, score.up())

                def attention_transposes(j):
                    pe.wait_ge(probs_ready, prb.due())
                    for a in range(j % QT + 1):
                        pe.transpose(b_s0[:, a * P:(a + 1) * P], prob[:, 0, a * P:(a + 1) * P], ident)
                        pe.transpose(b_s1[:, a * P:(a + 1) * P], prob[:, 1, a * P:(a + 1) * P], ident)
                    pe.transpose(b_cmp[0:NCMP, 0:P], pc[:, 0:NCMP], ident)\
                        .then_inc(probs_transposed, ptp.up())

                def attention_values(j):
                    g, i = j // QT, j % QT
                    rows = slice(g * DH, (g + 1) * DH)
                    if j == 0:
                        pe.wait_ge(attention_out_read, ofree.due())
                    col = slice(i * P, (i + 1) * P)
                    pe.matmul(b_o[rows, col], vc[0:NCMP, rows], ptc[0:NCMP, :], start=True, stop=False,
                              skip_group_check=True)
                    for a in range(i + 1):
                        pe.matmul(b_o[rows, col], vs[:, a, rows], pt[:, 0, a * P:(a + 1) * P],
                                  start=False, stop=False, skip_group_check=True)
                        ins = pe.matmul(b_o[rows, col], vw[:, a, rows], pt[:, 1, a * P:(a + 1) * P],
                                        start=False, stop=a == i, skip_group_check=True)
                    ins.then_inc(values_added, pv.up())

                def retention_products(j):
                    if j == 2:
                        pe.wait_ge(retention_input_ready, rin.due())
                        ret_scores(0, b_r0)
                        ret_scores(1, b_r1)
                    if j == 3:
                        pe.wait_ge(product_read, rfree.due())
                        ret_transposes(b_r0, tile_c)
                        pe.wait_ge(product_read, rfree.due())
                        ret_scores(2, b_r1)
                    if j == 4:
                        pe.wait_ge(product_read, rfree.due())
                        ret_scores(3, b_r0)
                        pe.wait_ge(product_read, rfree.due())
                        ret_transposes(b_r1, tile_b)
                    if j == 5:
                        pe.wait_ge(product_read, rfree.due(2))
                        ret_values(0, b_r0)
                        ret_values(1, b_r1)
                    if j == 6:
                        pe.wait_ge(product_read, rfree.due(2))
                        pe.wait_ge(retention_input_ready, rin.due())
                        pe.matmul(b_r0[:, :], ones, tile_c, start=True, stop=True)\
                            .then_inc(product_ready, rps.up())

                def beside(j, k):
                    if k == 3 and j > 2:
                        retention_products(j - 1)
                    if k == (5 if j % QT > 1 else 6):
                        attention_transposes(j)

                attention_scores(0)
                for j in range(RET_UNITS):
                    unit(u0, j, 2, [bank[j % 2][:, :]], a_op(), 8, lambda k, j=j: beside(j, k))
                    if j == 7:
                        square_sum()
                    pe.wait_ge(probs_copied, ptr.due())
                    if j < RET_UNITS - 1:
                        attention_scores(j + 1)
                    attention_values(j)

            first_lags = [2, 3, 3]

            def pairs(u0, n, rhs, nk, first=None):
                for j in range(n):
                    unit(u0, j, 2, [bank4(2 * j), bank4(2 * j + 1)], rhs, nk, first if j == 0 else None)

            def singles(u0, n, rhs, nk=8, first=None, lags=(), normed=False):
                for j in range(n):
                    unit(u0, j, lags[j] if j < len(lags) else 4, [bank4(j)], rhs, nk,
                         first if j == 0 else None)
                    if j == 0 and normed:
                        square_sum()

            pe.wait_ge(attention_out_read, ofree.now() + 1)
            pairs(U_YA, YA_UNITS, y_op(8), 4)
            for j in range(YB_UNITS):
                if j == 1:
                    pe.wait_ge(y_tile_ready, y_rdy.due(RH * 2))
                unit(U_YB, j, first_lags[j] if j < 3 else 4, [bank4(j)],
                     a_op() if j % 2 == 0 else y_op(), 8)
            merged = [8, 9, 10, 11, 4, 5, 6, 7]
            singles(U_MIX, MIX_UNITS, ((lambda k: y_hi[:, merged[k], :]), (lambda k: y_lo[:, merged[k], :])),
                    first=next_y)
            singles(U_FFN, 4, a_op(), first=next_a, normed=True)
            u, done = U_FFN, 4
            for c in FFN_CHUNKS:
                with repeat(pe, c // 2 - done // 4, []) as b:
                    singles(b * 4 + (u + done), 4, a_op())
                u, done = u + 2 * c, 0
                singles(u, 8, y_op(), c, first=next_y)
                u += 8
            square_sum()

            with repeat(pe, LAYERS, [(a_rdy, 24), (y_rdy, 54), (sums, 15), (sump, 15), (tin, 4),
                                     (tout, 4), (rin, 4), (rps, 4), (score, 16), (prb, 16),
                                     (ptp, 16), (ptr, 16), (pv, 16), (ofree, 4)]) as layer:
                ul = layer * L_UNITS + U_L
                def value_transposes(j):
                    result_transposes(ul, j, (b_cmp, b_o)[j % 2], kn[:, j, :])

                for j in range(4):
                    unit(ul, j, 4, [bank4(j)], a_op(), 8, next_a if j == 0 else None)
                    if j == 1:
                        square_sum()

                def attention_scores(s):
                    hd, i = s // QT, s % QT
                    n = (i + 1) * P
                    if i == 0:
                        pe.wait_ge(retention_input_ready, rin.due())
                    for e, dst in enumerate((b_s0, b_s1)):
                        rows = slice(64 * e, 64 * (e + 1))
                        ins = pe.matmul(dst[:, 0:n], qn[rows, hd, i * P:(i + 1) * P],
                                        kn[rows, hd, 0:n], start=True, stop=True)
                    ins.then_inc(scores_ready, score.up())

                def attention_values(s):
                    hd, i = s // QT, s % QT
                    pe.wait_ge(probs_ready, prb.due())
                    for a in range(i + 1):
                        ins = pe.transpose(b_cmp[:, a * P:(a + 1) * P], prob[:, 0, a * P:(a + 1) * P], ident)
                    ins.then_inc(probs_transposed, ptp.up())
                    if s < 15:
                        attention_scores(s + 1)
                    pe.wait_ge(probs_copied, ptr.due())
                    if i == 0:
                        pe.wait_ge(attention_out_read, ofree.due())
                    for a in range(i + 1):
                        ins = pe.matmul(b_o[:, i * P:(i + 1) * P], vn[:, hd, a, :],
                                        pt[:, 0, a * P:(a + 1) * P], start=a == 0, stop=a == i,
                                        skip_group_check=True)
                    ins.then_inc(values_added, pv.up())

                for j in range(8):
                    if j == 7:
                        pe.wait_ge(evac, ul + (L_QK + 10))
                        attention_scores(0)
                    unit(ul + L_QK, j, 4, [bank4(j)], a_op(), 8,
                         lambda k, j=j: square_sum((b_r0, b_r1)[(j - 1) % 2], ones2, (tile_b, tile_c)[(j - 1) % 2])
                         if k == 3 and j > 0 else None)
                    if j == 0:
                        value_transposes(0)
                        value_transposes(1)
                    if j == 2:
                        pe.wait_ge(evac, ul + (L_QK + 6))
                        value_transposes(2)
                        value_transposes(3)
                attention_values(0)

                def mixed(slot, k):
                    if k != 3:
                        return
                    if slot == 0:
                        square_sum(b_r1, ones2, tile_c)
                    elif slot % QT == 0:
                        square_sum(b_r0)
                    if 2 <= slot <= 5:
                        pe.wait_ge(to_transpose, tin.due())
                        g = slot - 2
                        pe.matmul(b_r1[:, :], par[:, C2_POOLW + g * P:C2_POOLW + (g + 1) * P],
                                  (tile_b, tile_d)[POOLED[g]], start=True, stop=True)\
                            .then_inc(product_ready, rps.up())

                for slot in range(16):
                    unit(ul + L_MIX, slot, 2, [bank[slot % 2][:, :]], a_op(), 8,
                         lambda k, slot=slot: mixed(slot, k))
                    if slot < 15:
                        attention_values(slot + 1)
                square_sum(b_r0)
                y_rdy.due(9)
                with repeat(pe, 3, [(y_rdy, 1)]) as br:
                    ub = ul + L_MERGE + br * 12
                    for half in range(2):
                        for j in range(4):
                            unit(ub, half * 6 + j, [2, 3, 3, 4][j], [bank4(j)], a_op(), 8)
                        if half == 0:
                            pe.wait_ge(y_tile_ready, y_rdy.due())
                        for j in range(2):
                            unit(ub, half * 6 + 4 + j, 3 - j, [bank4(2 * j), bank4(2 * j + 1)],
                                 ((lambda k: y_hi[:, bass.ds(br * 4 + k, 1), :].rearrange("p a s -> p (a s)")),
                                  (lambda k: y_lo[:, bass.ds(br * 4 + k, 1), :].rearrange("p a s -> p (a s)"))), 4)
                singles(ul + L_WO, 8, y_op(), first=next_y, lags=first_lags)
                uc = ul + L_MLP
                singles(uc, 8, a_op(), first=next_a, normed=True)
                y_rdy.due(2)
                singles(uc + 8, 8, y_op(), first=next_y)
                with repeat(pe, 3, [(y_rdy, 8)]) as c:
                    uc = ul + (L_MLP + 16) + c * 16
                    singles(uc, 8, a_op())
                    singles(uc + 8, 8, y_op(), first=next_y)
                for j in range(4):
                    unit(ul + L_PLE, j, 2, [bank4(2 * j), bank4(2 * j + 1)], y_op(8), 2)
                    if j == 0:
                        square_sum()
                singles(ul + L_PLE + 4, 8, a_op(), first=next_a, lags=first_lags)

        @block.vector
        def _(dve):
            V = dve
            V.sem_inc(evac, 4)
            V.sem_inc(attention_out_read, 1)
            steps = Count()
            a_rdy, y_rdy = Count(), Count()
            pre, res, root = Count(), Count(), Count()
            sums = Count()
            tin, tout = Count(), Count()
            cp = Count()
            score, mx, ex, prb, pv = (Count() for _ in range(5))
            pv.k = 1
            ofree = Count(1)
            rin, rps, rfree = Count(), Count(), Count()

            def bank4(j):
                return bank[(j + 2) % 4][:, :]

            def leave(u0, j, ins):
                ins.then_inc(evac, 1)
                V.wait_ge(evac, u0 + (j + 5))

            def arrive(u0, j):
                V.wait_ge(vector_step, steps.now())
                V.wait_ge(unit_done, u0 + (j + 5))

            def scaled(dst, src, u0, j):
                arrive(u0, j)
                leave(u0, j, V.tensor_tensor(dst, src, rstd[:, :], ALU.mult))

            def split(at, src):
                V.tensor_copy(y_hi[:, at, :], src).then_inc(vector_step, steps.up())
                V.wait_ge(vector_step, steps.now())
                V.tensor_tensor(y_lo[:, at, :], src, y_hi[:, at, :], ALU.subtract)\
                    .then_inc(y_tile_ready, y_rdy.up())
                V.wait_ge(y_tile_ready, y_rdy.now())

            def norm_tile(k, g_col, last):
                operand_tile(k, g_col)
                square_tile(k, last)

            def operand_tile(k, g_col):
                g = par[:, g_col + k:g_col + k + 1]
                V.tensor_scalar(a_hi[:, k, :], h[:, k, :], g, None, ALU.mult)\
                    .then_inc(vector_step, steps.up())
                V.wait_ge(vector_step, steps.now())
                V.scalar_tensor_tensor(out=a_lo[:, k, :], in0=h[:, k, :], scalar=g,
                                                in1=a_hi[:, k, :], op0=ALU.mult, op1=ALU.subtract)\
                                                    .then_inc(a_tile_ready, a_rdy.up())
                V.wait_ge(a_tile_ready, a_rdy.now())

            def square_tile(k, last, tmp=tile_a):
                V.tensor_tensor(tmp if k else ssum[:, :], h[:, k, :], h[:, k, :], ALU.mult)\
                    .then_inc(vector_step, steps.up())
                V.wait_ge(vector_step, steps.now())
                if k:
                    ins = V.tensor_tensor(ssum[:, :], ssum[:, :], tmp, ALU.add)
                    if last:
                        ins.then_inc(squares_ready, sums.up())
                        V.wait_ge(squares_ready, sums.now())
                    else:
                        ins.then_inc(vector_step, steps.up())
                        V.wait_ge(vector_step, steps.now())

            def rms():
                V.wait_ge(root_ready, root.due())
                V.reciprocal(rstd[:, :], rstd[:, :]).then_inc(vector_step, steps.up())
                V.wait_ge(vector_step, steps.now())

            def rope_in(src, u0, j, swap):
                scaled(tile_a, src, u0, j)
                V.sem_inc(wait_placed, 1)
                V.stream_shuffle(tile_b, tile_a, swap).then_inc(vector_step, steps.up())

            def rope_out(dst, cos, sin):
                V.wait_ge(vector_step, steps.now())
                V.tensor_tensor(tile_b, tile_b, sin, ALU.mult).then_inc(vector_step, steps.up())
                V.tensor_tensor(tile_a, tile_a, cos, ALU.mult).then_inc(vector_step, steps.up())
                V.wait_ge(vector_step, steps.now())
                return V.tensor_tensor(dst, tile_a, tile_b, ALU.add)

            V.memset(small[:, :], 0.0).then_inc(vector_step, steps.up())
            V.memset(ta[:, 0:16], 0.0).then_inc(vector_step, steps.up())
            V.memset(tb[:, 0:16], 0.0).then_inc(vector_step, steps.up())
            V.memset(td[:, 0:16], 0.0).then_inc(vector_step, steps.up())
            V.wait_ge(vector_step, steps.now())
            V.memset(eps, EPS).then_inc(to_activate, pre.up())
            V.wait_ge(to_activate, pre.now())
            V.wait_ge(first_gain_landed, 16)
            for k in range(KD):
                V.wait_ge(x_tile_landed[k], 16)
                operand_tile(k, C1_MIX)
            V.wait_ge(x_square_ready, KD)
            V.tensor_copy(small[:, 20:21], h[:, 0, 0:1]).then_inc(x_used, 1)
            rms()
            V.wait_ge(constants_landed, 32)
            V.wait_ge(parameters_landed, 16)
            for kv in range(2):
                scaled(tile_a, bank4(kv), 0, kv)
                t16 = tile_a.rearrange("p (c r) -> p c r", r=CMP_STRIDE)
                for g in range(KVG):
                    for par_ in range(2):
                        for half in range(2):
                            src = t16[g * DH:(g + 1) * DH, half:half + NCMP, par_::2]
                            V.tensor_copy(xc[par_ * DH:(par_ + 1) * DH, 8 * half:8 * half + 8, g, :],
                                               src.rearrange("p c r -> p r c"))\
                                                   .then_inc(vector_step, steps.up())
                V.wait_ge(vector_step, steps.now())
                pe_ = par[:, C1_PE + 16 * kv:C1_PE + 16 * kv + 16]
                xf = xc.rearrange("p m g c -> p m (g c)")
                V.tensor_tensor(xf, xf, pe_.unsqueeze(2).to_broadcast([P, 16, 2 * NCMP]), ALU.add)\
                    .then_inc(vector_step, steps.up())
                V.wait_ge(vector_step, steps.now())
                V.tensor_copy(xc_hi[kv], xc).then_inc(vector_step, steps.up())
                V.wait_ge(vector_step, steps.now())
                V.tensor_tensor(xc_lo[kv], xc, xc_hi[kv], ALU.subtract)\
                    .then_inc(y_tile_ready, y_rdy.up())
                V.wait_ge(y_tile_ready, y_rdy.now())
            def values(j):
                V.wait_ge(transposed, tout.due())
                V.tensor_copy((vs, vw)[j - 2], (b_r0, b_cmp)[j - 2][:, :].rearrange("p (a f) -> p a f", f=P))\
                    .then_inc(vector_step, steps.up())

            for j in (2, 3):
                scaled(prob[:, j - 2, :], bank4(j), 0, j)
            values(2)
            V.wait_ge(tables_landed, 32)
            for j in range(4, 10):
                dst = (ks, kw)[j - 4] if j < 6 else m[:, 3 + j - 6, :]
                rope_in(bank4(j), 0, j, SWAP_NSA)
                rope_out(dst, rope_cn, rope_sn).then_inc(vector_step, steps.up())
                if j == 4:
                    values(3)
            scaled(prob[:, 0, :], bank4(10), 0, 10)
            arrive(0, 11)
            leave(0, 11, V.tensor_copy(small[:, 21:22], bank4(11)[:, 0:1]))
            V.wait_ge(transposed, tout.due())
            V.tensor_copy(gn, b_r0[:, :].rearrange("p (i c) -> p i c", c=P)[:, :, 0:24])\
                .then_inc(to_activate, pre.up())
            V.wait_ge(to_activate, pre.now())
            def hidden_in(kv):
                arrive(U_CMP, kv * 4 + 3)
                V.tensor_copy(hidden_rows[kv][0:KVG * NCMP, 0:CMP_HIDDEN],
                              bank[kv][0:KVG * NCMP, 0:CMP_HIDDEN]).then_inc(evac, 4)
                V.wait_ge(evac, U_CMP + kv * 4 + 8)

            def hidden_out(kv):
                V.wait_ge(transposed, tout.due())
                V.tensor_copy(hid[:, :, 0:KVG * NCMP],
                              b_cmp[:, 0:128].rearrange("p (k c) -> p k c", c=64)[:, :, 0:KVG * NCMP])\
                    .then_inc(hidden_ready, 1)
                V.wait_ge(hidden_ready, kv + 1)

            hidden_in(0)
            hidden_out(0)
            hidden_in(1)
            V.wait_ge(compressed, cp.due())
            V.tensor_copy(kc[:, 0:NCMP], b_r0[:, 0:NCMP]).then_inc(vector_step, steps.up())
            hidden_out(1)
            V.wait_ge(compressed, cp.due())
            V.tensor_copy(vc[0:NCMP, :], b_r1[0:NCMP, 0:P]).then_inc(vector_step, steps.up())
            V.wait_ge(activated, res.due())

            def maxima(i, mask, scale, cmp=0):
                n = (i + 1) * P
                V.wait_ge(scores_ready, score.due())
                diag = scores[:, :, i * P:n]
                V.tensor_tensor(diag, diag, mask.unsqueeze(1).to_broadcast([P, 2, P]), ALU.add)\
                    .then_inc(vector_step, steps.up())
                if cmp:
                    V.tensor_tensor(b_cmp[:, 0:NCMP], b_cmp[:, 0:NCMP],
                                    cst[:, K_CMPA + i * NCMP:K_CMPA + (i + 1) * NCMP], ALU.add)\
                        .then_inc(vector_step, steps.up())
                V.wait_ge(vector_step, steps.now())
                V.tensor_reduce(small[:, 8 + cmp:10 + cmp], scores[:, :, 0:n], AX.X, ALU.max)\
                    .then_inc(vector_step, steps.up())
                if cmp:
                    V.tensor_reduce(small[:, 8:9], b_cmp[:, 0:NCMP], AX.X, ALU.max)\
                        .then_inc(vector_step, steps.up())
                V.wait_ge(vector_step, steps.now())
                b = 2 + cmp
                V.tensor_scalar(small[:, 0:b], small[:, 8:8 + b], -scale, None, ALU.mult)\
                    .then_inc(max_ready, mx.up())
                V.wait_ge(max_ready, mx.now())

            causal = cst[:, K_CAUSAL:K_CAUSAL + P]
            def row_tile(x, n):
                return x[:, bass.ds(n, 1), :].rearrange("p a s -> p (a s)")

            def next_query(t):
                V.tensor_copy(qt, row_tile(m, t + 3)).then_inc(to_transpose, tin.up())
                V.wait_ge(to_transpose, tin.now())

            def next_gates(t):
                for g in range(KVG):
                    V.tensor_copy(gates[:, :, 3 * g:3 * g + 3], gn[:, :, bass.ds(t * 3 + 12 * g, 3)])\
                        .then_inc(vector_step, steps.up())
                V.wait_ge(vector_step, steps.now())

            def step_maxima(j):
                maxima(j % QT, causal, DH ** -0.5, cmp=1)

            def step_probs(t, j):
                g, i = j // QT, j % QT
                n = (i + 1) * P
                V.wait_ge(exp_ready, ex.due())
                V.reciprocal(small[:, 12:15], small[:, 4:7]).then_inc(vector_step, steps.up())
                V.wait_ge(vector_step, steps.now())
                gate = [gates[:, i, 3 * g + b:3 * g + b + 1] for b in range(3)]
                V.scalar_tensor_tensor(out=pc[:, 0:NCMP], in0=pc[:, 0:NCMP], scalar=small[:, 12:13],
                                       in1=cst[:, K_CMPM + i * NCMP:K_CMPM + (i + 1) * NCMP],
                                       op0=ALU.mult, op1=ALU.mult).then_inc(vector_step, steps.up())
                V.tensor_scalar(prob[:, 0, 0:n], prob[:, 0, 0:n], small[:, 13:14], gate[1],
                                ALU.mult, ALU.mult).then_inc(vector_step, steps.up())
                V.wait_ge(vector_step, steps.now() - 1)
                V.tensor_scalar(pc[:, 0:NCMP], pc[:, 0:NCMP], gate[0], None, ALU.mult)\
                    .then_inc(vector_step, steps.up())
                V.tensor_scalar(prob[:, 1, 0:n], prob[:, 1, 0:n], small[:, 14:15], gate[2],
                                ALU.mult, ALU.mult).then_inc(probs_ready, prb.up())
                V.wait_ge(probs_ready, prb.now())

            def unit_in(t, j):
                u0 = t * RET_UNITS + U_RET
                src = bank[j % 2][:, :]
                if j < 2:
                    rope_in(src, u0, j, SWAP_RET)
                elif j in (2, 3):
                    dst = tile_c if j == 2 else tile_b
                    scaled(dst, src, u0, j)
                    V.tensor_copy(small[:, 20:21], dst[:, 0:1])\
                        .then_inc(retention_input_ready, rin.up())
                    V.wait_ge(retention_input_ready, rin.now())
                elif j in (4, 7):
                    scaled(row_tile(m, t * 2 + (j - 4) // 3), src, u0, j)
                else:
                    scaled(rg[:, j - 5, :], src, u0, j)

            p_at = [0, 512, 896, 1152, 1280]

            def decayed(t, a, src):
                n = S - a * P
                V.wait_ge(product_ready, rps.due())
                V.tensor_tensor(rp[:, p_at[a]:p_at[a + 1]], src[:, 0:n], row_tile(decay_t, t)[:, 0:n],
                                ALU.mult).then_inc(product_read, rfree.up())
                V.wait_ge(product_read, rfree.now())

            def value_rows(e, src):
                V.wait_ge(product_ready, rps.due())
                V.tensor_copy(rv[:, :, e * P:(e + 1) * P], src[:, :].rearrange("p (a f) -> p a f", f=P))\
                    .then_inc(product_read, rfree.up())
                V.wait_ge(product_read, rfree.now())

            def attention_out(t):
                V.wait_ge(values_added, pv.due(8))
                hi = row_tile(y_hi, t + 8)
                V.tensor_copy(hi, b_o[:, :]).then_inc(vector_step, steps.up())
                V.wait_ge(vector_step, steps.now())
                V.tensor_tensor(row_tile(y_lo, t + 8), b_o[:, :], hi, ALU.subtract)\
                    .then_inc(attention_out_read, ofree.up())
                V.wait_ge(attention_out_read, ofree.now())

            def inverse_root(t, half):
                if half == 0:
                    V.wait_ge(root_ready, root.due())
                    V.reciprocal(tile_c[:, 0:S // 2], tile_c[:, 0:S // 2])\
                        .then_inc(vector_step, steps.up())
                    return
                V.wait_ge(vector_step, steps.now())
                V.reciprocal(tile_c[:, S // 2:], tile_c[:, S // 2:]).then_inc(root_inverted, 1)
                V.wait_ge(root_inverted, t + 1)
                res.due()
                y_rdy.up(2)

            def outputs_in():
                V.wait_ge(product_ready, rps.due(2))
                V.tensor_copy(rq, b_r0[:, :]).then_inc(product_read, rfree.up())
                V.wait_ge(product_read, rfree.now())
                V.tensor_copy(rk, b_r1[:, :]).then_inc(product_read, rfree.up())
                V.wait_ge(product_read, rfree.now())
                V.tensor_tensor(tile_c, rq, rk, ALU.add).then_inc(retention_input_ready, rin.up())
                V.wait_ge(retention_input_ready, rin.now())

            def slot(t, j, last=None):
                step_maxima(j)
                if j == 7 and last is None:
                    next_query(t + 1)
                if j == 3:
                    V.wait_ge(y_tile_ready, y_rdy.now())
                if j > 0 and j != 6:
                    unit_in(t, j - 1)
                elif j == 0 and last is not None:
                    unit_in(last, 7)
                step_probs(t, j)
                if last is not None and j == 0:
                    attention_out(last)
                if last is not None and j == 1:
                    V.wait_ge(output_gated, last * 2 + 2)
                if j == 1:
                    rope_out(rq, rope_cr, rope_sr).then_inc(vector_step, steps.up())
                if j == 2:
                    rope_out(rk, rope_cr, rope_sr).then_inc(retention_input_ready, rin.up())
                    V.wait_ge(retention_input_ready, rin.now())
                if last is not None and j < 2:
                    inverse_root(last, j)
                if j == 3:
                    decayed(t, 0, b_r0)
                    decayed(t, 1, b_r1)
                if j == 4:
                    value_rows(0, b_r0)
                    decayed(t, 2, b_r1)
                if j == 5:
                    decayed(t, 3, b_r0)
                    value_rows(1, b_r1)
                if j == 6:
                    outputs_in()
                    unit_in(t, 5)
                if j == 7:
                    V.wait_ge(product_ready, rps.due())
                    if last is not None:
                        V.wait_ge(y_tile_ready, y_rdy.now())
                    V.tensor_copy(small[:, 24:26], par[:, bass.ds(t * 2 + C1_GN, 2)])\
                        .then_inc(vector_step, steps.up())
                    for o in (rq, rk):
                        V.scalar_tensor_tensor(out=o, in0=b_r0[:, :], scalar=-1.0 / RDV, in1=o,
                                               op0=ALU.mult, op1=ALU.add)\
                            .then_inc(vector_step, steps.up())
                    V.wait_ge(vector_step, steps.now())
                    V.tensor_tensor(tile_a, rq, rq, ALU.mult).then_inc(vector_step, steps.up())
                    V.tensor_tensor(ssum[:, :], rk, rk, ALU.mult).then_inc(vector_step, steps.up())
                    V.wait_ge(vector_step, steps.now())
                    V.tensor_tensor(ssum[:, :], ssum[:, :], tile_a, ALU.add)\
                        .then_inc(squares_ready, sums.up())
                    V.wait_ge(squares_ready, sums.now())
                    if last is None:
                        next_gates(t + 1)

            next_query(0)
            next_gates(0)
            for j in range(3):
                slot(0, j)
            with repeat(V, RH - 1, [(steps, N_RET), (score, 8), (mx, 8), (ex, 8), (prb, 8), (pv, 8),
                                    (ofree, 1), (rin, 4), (rps, 9), (rfree, 8), (sums, 1), (root, 1),
                                    (res, 1), (y_rdy, 2), (tin, 1)]) as t:
                for j in range(3, 8):
                    slot(t, j)
                for j in range(3):
                    slot(t + 1, j, t)
            for j in range(3, 8):
                slot(RH - 1, j, RH - 2)
            unit_in(RH - 1, 7)
            attention_out(RH - 1)
            V.tensor_copy(small[:, 21:22], m[:, 7, 0:1]).then_inc(to_activate, pre.up())
            for half in range(2):
                inverse_root(RH - 1, half)
            V.wait_ge(output_gated, 2 * RH)
            V.tensor_copy(small[:, 20:21], rq[:, 0:1]).then_inc(tables_used, 1)
            V.wait_ge(to_activate, pre.now())

            V.wait_ge(activated, res.due(2))
            for j in range(YA_UNITS):
                arrive(U_YA, j)
                for o in range(2):
                    n = 2 * j + o
                    ins = V.tensor_tensor(m[:, n, :], bank4(n), m[:, n, :], ALU.mult)
                    if o == 0:
                        ins.then_inc(vector_step, steps.up())
                leave(U_YA, j, ins)
            merged = [8, 9, 10, 11, 4, 5, 6, 7]
            for n in range(KD):
                scaled(tile_a, bank4(2 * n), U_YB, 2 * n)
                V.wait_ge(activated, res.due())
                arrive(U_YB, 2 * n + 1)
                leave(U_YB, 2 * n + 1, V.tensor_tensor(tile_b, bank4(2 * n + 1), tile_a, ALU.mult))
                V.tensor_tensor(m[:, n, :], m[:, n, :], tile_b, ALU.add)\
                    .then_inc(vector_step, steps.up())
                V.wait_ge(vector_step, steps.now())
                if n == 0:
                    V.wait_ge(y_tile_ready, y_rdy.now())
                if n < 4:
                    split(merged[n], m[:, n, :])
            for n in range(4, KD):
                split(merged[n], m[:, n, :])
            V.wait_ge(x_landed, 16)

            def residual(u0, j, n, g_col=None):
                arrive(u0, j)
                leave(u0, j, V.tensor_tensor(h[:, n, :], bank4(j), h[:, n, :], ALU.add))
                if g_col is not None:
                    norm_tile(n, g_col, n == KD - 1)

            for n in range(KD):
                residual(U_MIX, n, n, C1_FFN)
            rms()
            V.memset(ssum[:, 0:1], 0.0).then_inc(vector_step, 1)
            steps.k += 1
            u = U_FFN
            tile0 = 0
            for c in FFN_CHUNKS:
                with repeat(V, c // 2, [(steps, 14), (pre, 2), (res, 2), (y_rdy, 2)]) as b:
                    for j in range(2):
                        hidden = b * 2 + (tile0 + j)
                        for gv in range(2):
                            buf, flat = ((ta, tile_a), (tb, tile_b))[gv]
                            scaled(flat, bank4(2 * j + gv), b * 4 + u, 2 * j + gv)
                            dst = (tile_c, tile_d)[gv]
                            cw = [par[:, bass.ds(hidden * 4 + (C1_CONV + gv * FT * 4 + x), 1)] for x in range(4)]
                            V.tensor_scalar(dst, flat, cw[2], cw[3], ALU.mult, ALU.add)\
                                .then_inc(vector_step, steps.up())
                            V.wait_ge(vector_step, steps.now())
                            V.scalar_tensor_tensor(out=dst, in0=buf[:, 15:15 + S], scalar=cw[1], in1=dst,
                                                        op0=ALU.mult, op1=ALU.add)\
                                                            .then_inc(vector_step, steps.up())
                            V.wait_ge(vector_step, steps.now())
                            ins = V.scalar_tensor_tensor(out=dst, in0=buf[:, 14:14 + S], scalar=cw[0],
                                                         in1=dst, op0=ALU.mult, op1=ALU.add)
                            if gv == 0:
                                ins.then_inc(to_activate, pre.up())
                                V.wait_ge(to_activate, pre.now())
                            else:
                                ins.then_inc(vector_step, steps.up())
                                V.wait_ge(vector_step, steps.now())
                        V.wait_ge(activated, res.due())
                        V.tensor_tensor(tile_d, tile_d, tile_c, ALU.mult)\
                            .then_inc(vector_step, steps.up())
                        V.wait_ge(vector_step, steps.now())
                        yt = b * 2 + j
                        hi = y_hi[:, bass.ds(yt, 1), :].rearrange("p a s -> p (a s)")
                        V.tensor_copy(hi, tile_d).then_inc(vector_step, steps.up())
                        V.wait_ge(vector_step, steps.now())
                        V.tensor_tensor(y_lo[:, bass.ds(yt, 1), :].rearrange("p a s -> p (a s)"),
                                                 tile_d, hi, ALU.subtract)\
                                                     .then_inc(y_tile_ready, y_rdy.up())
                        V.wait_ge(y_tile_ready, y_rdy.now())
                u += 2 * c
                tile0 += c
                for n in range(KD):
                    residual(u, n, n)
                    if tile0 == FT:
                        square_tile(n, n == KD - 1)
                u += 8
            rms()
            for k in range(KD):
                V.scalar_tensor_tensor(out=h[:, k, :], in0=h[:, k, :],
                                       scalar=par[:, C1_FIN + k:C1_FIN + k + 1],
                                       in1=rstd[:, :], op0=ALU.mult, op1=ALU.mult)\
                    .then_inc(h_tile_ready, 1)
            V.wait_ge(h_tile_ready, KD)
            V.tensor_copy(small[:, 20:21], par[:, 0:1]).then_inc(parameters_used, 1)
            V.wait_ge(parameters_used, 1)

            chunk = cst[:, K_CHUNK:K_CHUNK + P]
            V.wait_ge(gains_landed, 16 * LAYERS)
            hi_rdy, hready = Count(), Count(KD)
            with repeat(V, LAYERS, [(steps, N_LAYER), (a_rdy, 24), (y_rdy, 54), (pre, 1), (res, 33),
                                    (root, 15), (sums, 15), (tin, 4), (tout, 4), (rin, 4), (rps, 4),
                                    (score, 16), (mx, 16), (ex, 16), (prb, 16), (pv, 16),
                                    (ofree, 4), (hi_rdy, KD), (hready, KD)]) as layer:
                ul = layer * L_UNITS + U_L
                sums.up()
                for k in range(KD):
                    V.wait_ge(hi_tile_ready, hi_rdy.due())
                    V.scalar_tensor_tensor(out=a_lo[:, k, :], in0=h[:, k, :],
                                           scalar=mix_gain[:, bass.ds(layer * KD + k, 1)],
                                           in1=a_hi[:, k, :], op0=ALU.mult, op1=ALU.subtract)\
                        .then_inc(a_tile_ready, a_rdy.up())
                V.wait_ge(a_tile_ready, a_rdy.now())
                V.wait_ge(parameters_landed, layer * 16 + 32)
                rms()
                for e in range(2):
                    l0 = C2_LAM + 128 * e
                    V.tensor_tensor(tile_b[:, 0:64], par[:, l0:l0 + 64], par[:, l0 + 64:l0 + 128], ALU.mult)\
                        .then_inc(vector_step, steps.up())
                    V.wait_ge(vector_step, steps.now())
                    ins = V.tensor_reduce(small[:, 16 + e:17 + e], tile_b[:, 0:64], AX.X, ALU.add)
                    if e == 0:
                        ins.then_inc(vector_step, steps.up())
                        V.wait_ge(vector_step, steps.now())
                ins.then_inc(to_activate, pre.up())
                V.wait_ge(to_activate, pre.now())
                V.wait_ge(activated, res.due())
                linit = par[:, C2_LINIT:C2_LINIT + 1]
                V.tensor_scalar(small[:, 18:19], small[:, 17:18], small[:, 16:17], linit,
                                     ALU.subtract, ALU.subtract).then_inc(vector_step, steps.up())
                V.tensor_scalar(small[:, 19:20], linit, -1.0, 1.0, ALU.mult, ALU.add)\
                    .then_inc(vector_step, steps.up())
                V.wait_ge(vector_step, steps.now())
                V.tensor_tensor(small[:, 19:20], small[:, 19:20], par[:, C2_SUB:C2_SUB + 1], ALU.mult)\
                    .then_inc(vector_step, steps.up())
                V.wait_ge(vector_step, steps.now())
                def copy_values(j):
                    V.wait_ge(transposed, tout.due())
                    V.tensor_copy(vn[:, j], (b_cmp, b_o)[j % 2][:, :].rearrange("p (a f) -> p a f", f=P))\
                        .then_inc(vector_step, steps.up())

                for j in range(4):
                    scaled(kn[:, j, :], bank4(j), ul, j)
                value, square = (tile_a, tile_d), (tile_b, tile_c)

                def qk_in(j):
                    x, sq = value[j % 2], square[j % 2]
                    scaled(x, bank4(j), ul + L_QK, j)
                    V.tensor_tensor(sq, x, x, ALU.mult).then_inc(squares_ready, sums.up())
                    V.wait_ge(squares_ready, sums.now())

                def qk_out(j):
                    x, root_tile = value[j % 2], square[j % 2]
                    V.wait_ge(root_ready, root.due())
                    V.reciprocal(root_tile, root_tile).then_inc(vector_step, steps.up())
                    V.wait_ge(vector_step, steps.now())
                    gq = (C2_QG, C2_KG)[j % 2]
                    ins = V.scalar_tensor_tensor(out=(qn, kn)[j % 2][:, j // 2, :], in0=x,
                                                 scalar=par[:, gq:gq + 1], in1=root_tile,
                                                 op0=ALU.mult, op1=ALU.mult)
                    if j % 2:
                        ins.then_inc(retention_input_ready, rin.up())
                        V.wait_ge(retention_input_ready, rin.now())
                    else:
                        ins.then_inc(vector_step, steps.up())

                def head_inverse(c, parts=2):
                    if c == 0:
                        V.wait_ge(root_ready, root.due())
                    cols = slice(c * S // parts, (c + 1) * S // parts)
                    V.reciprocal(ssum[:, cols], ssum[:, cols]).then_inc(vector_step, steps.up())

                def head_out(hd):
                    V.wait_ge(vector_step, steps.now())
                    V.scalar_tensor_tensor(out=tile_c, in0=tile_c, scalar=small[:, 19:20],
                                           in1=ssum[:, :], op0=ALU.mult, op1=ALU.mult)\
                        .then_inc(vector_step, steps.up())
                    V.wait_ge(vector_step, steps.now())
                    split(8 + hd, tile_c)

                def step_maxima(s):
                    maxima(s % QT, chunk, 64 ** -0.5)

                def step_probs(s):
                    n = (s % QT + 1) * P
                    V.wait_ge(exp_ready, ex.due())
                    V.reciprocal(small[:, 12:14], small[:, 4:6]).then_inc(vector_step, steps.up())
                    V.wait_ge(vector_step, steps.now())
                    V.tensor_scalar(prob[:, 1, 0:n], prob[:, 1, 0:n], small[:, 13:14], small[:, 18:19],
                                    ALU.mult, ALU.mult).then_inc(vector_step, steps.up())
                    V.wait_ge(vector_step, steps.now())
                    V.scalar_tensor_tensor(out=prob[:, 0, 0:n], in0=prob[:, 0, 0:n],
                                                  scalar=small[:, 12:13], in1=prob[:, 1, 0:n],
                                                  op0=ALU.mult, op1=ALU.add)\
                                                      .then_inc(probs_ready, prb.up())
                    V.wait_ge(probs_ready, prb.now())

                def pooled_out(g):
                    V.wait_ge(product_ready, rps.due())
                    scale = par[:, C2_PSCALE + g:C2_PSCALE + g + 1]
                    V.tensor_scalar(y_hi[:, g, :], b_r1[:, :], scale, None, ALU.mult)\
                        .then_inc(vector_step, steps.up())
                    V.wait_ge(vector_step, steps.now())
                    V.scalar_tensor_tensor(out=y_lo[:, g, :], in0=b_r1[:, :], scalar=scale,
                                           in1=y_hi[:, g, :], op0=ALU.mult, op1=ALU.subtract)\
                        .then_inc(y_tile_ready, y_rdy.up())
                    V.wait_ge(y_tile_ready, y_rdy.now())

                def mix_in(j):
                    scaled(tile_b if 4 <= j < 12 and j % 2 else tile_a, bank[j % 2][:, :],
                           ul + L_MIX, j)

                def mix(j):
                    if j < 4:
                        x, w = ta, 1
                        for lev in range(j + 1):
                            y = (tb, td)[lev % 2]
                            V.tensor_tensor(y[:, 16:], x[:, 16:], x[:, 16 - w:16 - w + S], ALU.add)\
                                .then_inc(vector_step, steps.up())
                            V.wait_ge(vector_step, steps.now())
                            x, w = y, 2 * w
                        y = (tb, td)[(j + 1) % 2]
                        cnt = cst[:, K_CNT + 16 * j:K_CNT + 16 * (j + 1)]
                        V.scalar_tensor_tensor(out=y[:, 16:], in0=x[:, 16:], scalar=1.0 / w, in1=tile_a,
                                                    op0=ALU.mult, op1=ALU.subtract)\
                                                        .then_inc(vector_step, steps.up())
                        V.wait_ge(vector_step, steps.now())
                        V.tensor_tensor(y[:, 16:32], x[:, 16:32], cnt, ALU.mult)\
                            .then_inc(vector_step, steps.up())
                        V.wait_ge(vector_step, steps.now())
                        V.tensor_tensor(y[:, 16:32], y[:, 16:32], ta[:, 16:32], ALU.subtract)\
                            .then_inc(to_transpose, tin.up())
                        V.wait_ge(to_transpose, tin.now())
                    elif j < 12 and j % 2 == 0:
                        return
                    elif j < 12:
                        c = (j - 4) // 2
                        V.tensor_tensor(tile_d, tile_b, tile_a, ALU.mult)\
                            .then_inc(vector_step, steps.up())
                        V.wait_ge(vector_step, steps.now())
                        cw = [par[:, C2_CONV + 3 * c + x:C2_CONV + 3 * c + x + 1] for x in range(3)]
                        V.tensor_scalar(tile_b, tile_d, cw[2], None, ALU.mult)\
                            .then_inc(vector_step, steps.up())
                        V.wait_ge(vector_step, steps.now())
                        V.scalar_tensor_tensor(out=tile_b, in0=td[:, 15:15 + S], scalar=cw[1], in1=tile_b,
                                                    op0=ALU.mult, op1=ALU.add)\
                                                        .then_inc(vector_step, steps.up())
                        V.wait_ge(vector_step, steps.now())
                        V.scalar_tensor_tensor(out=m[:, c, :], in0=td[:, 14:14 + S], scalar=cw[0], in1=tile_b,
                                                    op0=ALU.mult, op1=ALU.add)\
                                                        .then_inc(vector_step, steps.up())
                        V.wait_ge(vector_step, steps.now())
                    else:
                        c = j - 12
                        V.tensor_tensor(tile_a, tile_a, m[:, c, :], ALU.mult)\
                            .then_inc(vector_step, steps.up())
                        V.wait_ge(vector_step, steps.now())
                        split(4 + c, tile_a)

                def attention_out():
                    V.wait_ge(values_added, pv.due(4))
                    V.tensor_copy(tile_c, b_o[:, :]).then_inc(attention_out_read, ofree.up())
                    V.wait_ge(attention_out_read, ofree.now())
                    V.wait_ge(attention_out_read, ofree.now())
                    V.tensor_tensor(ssum[:, :], tile_c, tile_c, ALU.mult)\
                        .then_inc(squares_ready, sums.up())
                    V.wait_ge(squares_ready, sums.now())

                for j in range(8):
                    if j == 7:
                        step_maxima(0)
                    if j > 0:
                        qk_in(j - 1)
                    if j == 7:
                        step_probs(0)
                    if j in (1, 3):
                        copy_values(j - 1)
                        copy_values(j)
                    if j > 1:
                        qk_out(j - 2)
                for k in range(16):
                    if k < 15:
                        step_maxima(k + 1)
                    if k == 0:
                        qk_in(7)
                    else:
                        mix_in(k - 1)
                    if k < 15:
                        step_probs(k + 1)
                    if k % QT == 3:
                        attention_out()
                    if k < 2:
                        qk_out(6 + k)
                    if 2 <= k <= 5:
                        pooled_out(k - 2)
                    if k > 0:
                        mix(k - 1)
                    if k >= 4 and k % QT < 2:
                        head_inverse(k % QT)
                    if k > 4 and k % QT == 2:
                        head_out(k // QT - 1)
                mix_in(15)
                mix(15)
                head_inverse(0, 1)
                head_out(3)
                for br in range(3):
                    ub = ul + (L_MERGE + br * 12)
                    for half in range(2):
                        for j in range(4):
                            scaled(work[:, j * S:(j + 1) * S], bank4(j), ub, half * 6 + j)
                        V.wait_ge(activated, res.due(4))
                        for j in range(2):
                            arrive(ub, half * 6 + 4 + j)
                            for o in range(2):
                                n = 2 * j + o
                                g = work[:, n * S:(n + 1) * S]
                                dst = m[:, half * 4 + n, :] if br == 0 else (tile_a, tile_b)[o]
                                ins = V.tensor_tensor(dst, bank4(n), g, ALU.mult)
                                if o == 0:
                                    ins.then_inc(vector_step, steps.up())
                            leave(ub, half * 6 + 4 + j, ins)
                            if br > 0:
                                V.wait_ge(vector_step, steps.now())
                                for o in range(2):
                                    n = half * 4 + 2 * j + o
                                    V.tensor_tensor(m[:, n, :], m[:, n, :], (tile_a, tile_b)[o], ALU.add)\
                                        .then_inc(vector_step, steps.up())
                                V.wait_ge(vector_step, steps.now())
                            if br == 2:
                                for o in range(2):
                                    split(half * 4 + 2 * j + o, m[:, half * 4 + 2 * j + o, :])
                for n in range(KD):
                    residual(ul + L_WO, n, n, C2_MLP)
                rms()
                V.wait_ge(p_landed, layer * 16 + 16)
                for k in range(2):
                    split(8 + k, prob[:, k, :])

                def mlp_chunk(uc, g_col=None):
                    for j in range(8):
                        arrive(uc, j)
                        leave(uc, j, V.scalar_tensor_tensor(out=tile_a, in0=bank4(j), scalar=0.0, in1=rstd[:, :],
                                                            op0=ALU.max, op1=ALU.mult))
                        V.tensor_tensor(tile_a, tile_a, tile_a, ALU.mult)\
                            .then_inc(vector_step, steps.up())
                        V.wait_ge(vector_step, steps.now())
                        split(j, tile_a)
                    for n in range(KD):
                        residual(uc + 8, n, n, g_col)

                V.sem_inc(wait_placed, 1)
                with repeat(V, 3, [(steps, 16), (y_rdy, 8)]) as c:
                    mlp_chunk(ul + L_MLP + c * 16)
                mlp_chunk(ul + (L_MLP + 48), C2_PLE)
                for j in range(4):
                    arrive(ul + L_PLE, j)
                    for o in range(2):
                        ins = V.tensor_copy(m[:, 2 * j + o, :], bank4(2 * j + o))
                        if o == 0:
                            ins.then_inc(vector_step, steps.up())
                    leave(ul + L_PLE, j, ins)
                    if j == 1:
                        rms()

                def ple_out(n):
                    g = (tile_a, tile_b)[n % 2]
                    V.wait_ge(activated, res.due())
                    V.tensor_tensor(g, g, m[:, n, :], ALU.mult).then_inc(vector_step, steps.up())
                    V.wait_ge(vector_step, steps.now())
                    V.tensor_tensor(h[:, n, :], h[:, n, :], g, ALU.add)\
                        .then_inc(h_tile_ready, hready.up())
                    V.wait_ge(h_tile_ready, hready.now())

                for n in range(KD):
                    scaled((tile_a, tile_b)[n % 2], bank4(n), ul + L_PLE + 4, n)
                    ple_out(n)
                V.tensor_copy(small[:, 20:21], par[:, 0:1]).then_inc(parameters_used, 1)
                V.wait_ge(parameters_used, layer + 2)


def _tables():
    f = np.float32
    tok = np.arange(S, dtype=f)

    def angles(half, theta):
        inv = np.power(f(theta), -np.arange(half, dtype=f) / f(half)).astype(f)
        return (tok[None, :] * inv[:, None]).astype(f)

    rope = np.zeros((P, 4, S), f)
    half = ROPE_DIM // 2
    a = angles(half, ROPE_THETA)
    rope[:, 0] = 1.0
    for p in range(P):
        d = p % DH
        if d < 2 * half:
            rope[p, 0] = np.cos(a[d % half])
            rope[p, 1] = np.sin(a[d % half]) * (-1 if d < half else 1)
    a = angles(RDK // 2, RET_THETA)
    for p in range(P):
        d, second = 16 * (p // 32) + p % 16, p % 32 >= 16
        rope[p, 2] = np.cos(a[d])
        rope[p, 3] = np.sin(a[d]) * (1 if second else -1)
    decay = np.zeros((P, RH, S), np.float64)
    dist = np.arange(S)[None, :] - np.arange(P)[:, None]
    for hd in range(RH):
        gamma = 1.0 - 2.0 ** (-5.0 - hd)
        decay[:, hd] = np.where(dist >= 0, gamma ** np.maximum(dist, 0), 0.0) * RDK ** -0.5
    cst = np.zeros((P, K_N), f)
    cst[:, K_ID:K_ID + P] = np.eye(P)
    cst[:, K_ONE:K_ONE + P] = 1.0
    cst[0:64, K_BD:K_BD + 64] = 1.0
    cst[64:, K_BD + 64:K_BD + P] = 1.0
    q, k = np.arange(P)[:, None], np.arange(P)[None, :]
    cst[:, K_CAUSAL:K_CAUSAL + P] = np.where(k <= q, 0.0, NEG)
    cst[:, K_CHUNK:K_CHUNK + P] = np.where(k // 64 <= q // 64, 0.0, NEG)
    for i in range(QT):
        seen = CMP_STRIDE * np.arange(NCMP)[None, :] + CMP_BLOCK - 1 <= i * P + q
        cst[:, K_CMPA + i * NCMP:K_CMPA + (i + 1) * NCMP] = np.where(seen, 0.0, NEG)
        cst[:, K_CMPM + i * NCMP:K_CMPM + (i + 1) * NCMP] = seen
    for g, w in enumerate(POOL_WINDOWS):
        cst[:, K_CNT + 16 * g:K_CNT + 16 * (g + 1)] = 1.0 / np.minimum(np.arange(16) + 1, w)
    return cst, decay.astype(f), rope


def _unit(w, tiles):
    out = np.zeros((P, 8, P), np.float32)
    for at, (k, n) in enumerate(tiles):
        part = w[k * P:(k + 1) * P, n * P:(n + 1) * P]
        out[:, at, :part.shape[1]] = part
    return out.reshape(P, UNIT)


def _full(w, n, k0=0, nk=8):
    return _unit(w, [(k0 + k, n) for k in range(nk)])


def _cols(w, tiles):
    return np.asarray(w).reshape(tiles, P).T


def _stream(x):
    units = []
    w = x["w_in"][0]
    at = np.cumsum([0, 512, 768, 24, 512, 512, 1024, 1024, 2048])
    q_nsa, kv, g_nsa, q_ret, k_ret, v_ret, g_ret, g_m = (w[:, a:b] for a, b in zip(at[:-1], at[1:]))
    heads = q_nsa.reshape(D, HEADS, DH)
    q_nsa = np.concatenate([heads[:, [t, HEADS // 2 + t]].reshape(D, P) for t in range(4)], axis=1)
    perm = np.concatenate([np.r_[16 * j:16 * j + 16, 64 + 16 * j:80 + 16 * j] for j in range(4)])
    perm = np.concatenate([hd * RDK + perm for hd in range(RH)])
    q_ret, k_ret = q_ret[:, perm], k_ret[:, perm]
    units += [_full(kv, n) for n in (0, 1, 3, 5, 2, 4)]
    units += [_full(q_nsa, n) for n in range(4)] + [_full(g_nsa, 0), np.zeros((P, UNIT), np.float32)]
    for w1 in (x["cmp_w1_k"][0], x["cmp_w1_v"][0]):
        units += [_unit(w1, [(4 * q + k, n) for k in range(4) for n in range(2)]) for q in range(4)]
    for hd in range(RH):
        units += [_full(q_ret, hd), _full(k_ret, hd), _full(v_ret, 2 * hd), _full(v_ret, 2 * hd + 1)]
        units += [_full(g_m, 2 * hd), _full(g_ret, 2 * hd), _full(g_ret, 2 * hd + 1), _full(g_m, 2 * hd + 1)]

    def two(w, j, nk):
        return _unit(w, [(k, 2 * j + o) for o in range(2) for k in range(nk)])
    rows = x["w_nsa_branch"][0].reshape(HEADS, DH, D)
    w_nsa = np.concatenate([rows[[t, HEADS // 2 + t]].reshape(P, D) for t in range(4)])
    units += [two(w_nsa, j, 4) for j in range(4)]
    for n in range(KD):
        units += [_full(g_m, 8 + n), _full(x["w_ret_branch"][0], n)]
    units += [_full(x["w_mix_out"][0], n) for n in range(KD)]
    up, down, t0 = x["w_ffn_up"][0], x["w_ffn_down"][0], 0
    for c in FFN_CHUNKS:
        for b in range(c):
            units += [_full(up, t0 + b), _full(up, FT + t0 + b)]
        units += [_full(down, n, t0, c) for n in range(KD)]
        t0 += c
    for i in range(LAYERS):
        w = x["w_in_2"][i]
        a, cx, cb, cc, q, k, v = (w[:, 512 * j:512 * (j + 1)] for j in range(7))
        gates = w[:, 3584:]
        units += [_full(v, n) for n in range(4)]
        for n in range(4):
            units += [_full(q, n), _full(k, n)]
        units += [_full(a, n) for n in range(4)]
        for n in range(4):
            units += [_full(cx, n), _full(cc, n)]
        units += [_full(cb, n) for n in range(4)]
        for br, wo in enumerate(("w_pool_out_2", "w_conv_out_2", "w_attn_out_2")):
            for half in range(2):
                units += [_full(gates, br * 8 + half * 4 + n) for n in range(4)]
                units += [two(x[wo][i], half * 2 + j, 4) for j in range(2)]
        units += [_full(x["w_o_2"][i], n) for n in range(KD)]
        for c in range(4):
            units += [_full(x["w_up_2"][i], 8 * c + n) for n in range(KD)]
            units += [_full(x["w_down_2"][i], n, 8 * c) for n in range(KD)]
        units += [two(x["w_ple_proj_2"][i], j, 2) for j in range(4)]
        units += [_full(x["w_ple_gate_2"][i], n) for n in range(KD)]
    assert len(units) == UNITS, (len(units), UNITS)
    both = np.stack(units).reshape(UNITS // 2, 2, P, UNIT)
    return np.ascontiguousarray(both.transpose(0, 2, 1, 3)).reshape(UNITS // 2, P, BLOCK)


def _parameters(x):
    p1 = np.zeros((P, C1_N), np.float32)
    p1[:, C1_MIX:C1_MIX + 8] = _cols(x["norm_mix_w"][0], KD)
    p1[:, C1_FFN:C1_FFN + 8] = _cols(x["norm_ffn_w"][0], KD)
    p1[:, C1_FIN:C1_FIN + 8] = _cols(x["norm_final_w"], KD)
    p1[:, C1_GN:C1_GN + 8] = _cols(x["ret_gn_w"][0], 2 * RH)
    conv = p1[:, C1_CONV:C1_PE].reshape(P, 2 * FT, 4)
    for j in range(3):
        conv[:, :, j] = _cols(x["ffn_conv_w"][0, j], 2 * FT)
    conv[:, :, 3] = _cols(x["ffn_conv_b"][0], 2 * FT)
    for kv, (pe, w2) in enumerate((("cmp_pe_k", "cmp_w2_k"), ("cmp_pe_v", "cmp_w2_v"))):
        p1[:, C1_PE + 16 * kv:C1_PE + 16 * kv + 16] = _cols(x[pe][0], 16)
        p1[:, C1_W2 + 128 * kv:C1_W2 + 128 * (kv + 1)] = x[w2][0].reshape(2, P, DH).transpose(1, 0, 2).reshape(P, P)
    p2 = np.zeros((LAYERS, P, C2_N), np.float32)
    for i in range(LAYERS):
        p = p2[i]
        p[:, C2_MIX:C2_MIX + 8] = _cols(x["norm_mix_g_2"][i], KD)
        p[:, C2_MLP:C2_MLP + 8] = _cols(x["norm_mlp_g_2"][i], KD)
        p[:, C2_PLE:C2_PLE + 8] = _cols(x["norm_ple_g_2"][i], KD)
        p[:, C2_PSCALE:C2_PSCALE + 4] = _cols(x["pool_scale_2"][i], PH)
        conv = p[:, C2_CONV:C2_CONV + 12].reshape(P, 4, 3)
        for j in range(3):
            conv[:, :, j] = _cols(x["conv_w_2"][i, j], 4)
        p[:, C2_QG] = np.tile(x["q_norm_g_2"][i], 2)
        p[:, C2_KG] = np.tile(x["k_norm_g_2"][i], 2)
        p[:, C2_SUB] = x["sub_norm_g_2"][i]
        p[:, C2_LINIT] = 0.8 - 0.6 * np.exp(-0.3 * i)
        for j, name in enumerate(("lam_q1_2", "lam_k1_2", "lam_q2_2", "lam_k2_2")):
            p[:, C2_LAM + 64 * j:C2_LAM + 64 * (j + 1)] = x[name][i][None, :]
        p[:, C2_POOLW:C2_POOLW + PH * P] = x["pool_w_2"][i].transpose(1, 0, 2).reshape(P, PH * P)
    return p1, p2


def _turned(a):
    return np.ascontiguousarray(a.T.reshape(-1, P, S).transpose(1, 0, 2))


def kernel(**inputs):
    import concourse.bacc as bacc
    from concourse.bass_utils import run_bass_kernel_spmd

    x = {name: np.asarray(a) for name, a in inputs.items()}
    cst, decay, rope = _tables()
    par1, par2 = _parameters(x)
    arrays = {
        "stream": _stream(x), "xT": _turned(x["x"][0]), "tab": cst, "decay": decay, "rope": rope,
        "par1": par1, "par2": par2, "pT": np.stack([_turned(p[0]) for p in x["p_2"]]),
    }
    nc = bacc.Bacc("TRN2", target_bir_lowering=False, num_devices=1)
    args = [nc.dram_tensor(name, a.shape, F32, kind="ExternalInput").ap() for name, a in arrays.items()]
    out = nc.dram_tensor("outT", (P, KD, S), F32, kind="ExternalOutput").ap()
    build(nc, *args, out)
    r = run_bass_kernel_spmd(nc, [arrays], core_ids=[0])
    got = np.asarray(r.results[0]["outT"])
    return np.ascontiguousarray(got.transpose(1, 0, 2).reshape(D, S).T).reshape(1, S, D)
```
